# Optimizing a Trainium2 kernel written in Bass

```python
import jax, jax.numpy as jnp
from jax import lax
import numpy as np

D_MODEL = 2048
BATCH = 1
SEQ = 256
DEPTH = 2

MLSTM_HEADS = 4
MLSTM_DK = 128
MLSTM_DV = 256
CONV_WIDTH = 4
GLA_HEADS = 4
GLA_DK = 128
GLA_DV = 256
GLA_GATE_RANK = 16
GLA_GATE_TAU = 16.0
CHUNK = 64
ATTN_HEADS = 16
ATTN_KV_HEADS = 4
ATTN_DH = 128
ROPE_DIM = ATTN_DH // 4
ROPE_THETA = 500000.0
IDX_HEADS = 16
IDX_DH = 64
IDX_ROPE_DIM = IDX_DH // 4
INDEX_TOPK = 256
Q_BLOCK = 128
N_EXPERTS = 16
N_GROUPS = 4
EXPERTS_PER_GROUP = N_EXPERTS // N_GROUPS
GROUP_SCORE_TOPK = 2
TOP_K_EXPERTS = 2
EXPERT_FF = 512
DEEPNORM_ALPHA = (2 * DEPTH) ** 0.25
DEEPNORM_BETA = (8 * DEPTH) ** -0.25
LN_EPS = 1e-5
HEAD_NORM_EPS = 1e-6
MAX_POS_OFFSET = 4096

N_EVEN = (DEPTH + 1) // 2
N_ODD = DEPTH // 2
EVEN_SPLITS = (MLSTM_HEADS * MLSTM_DK, MLSTM_HEADS * MLSTM_DK, MLSTM_HEADS * MLSTM_DV, MLSTM_HEADS, MLSTM_HEADS, MLSTM_HEADS * MLSTM_DV, GLA_HEADS * GLA_DK, GLA_HEADS * GLA_DK, GLA_HEADS * GLA_DV, GLA_GATE_RANK, GLA_HEADS * GLA_DV)
EVEN_IN = sum(EVEN_SPLITS)
MIX_WIDTH = MLSTM_HEADS * MLSTM_DV + GLA_HEADS * GLA_DV
ODD_SPLITS = (ATTN_HEADS * ATTN_DH, ATTN_KV_HEADS * ATTN_DH, ATTN_KV_HEADS * ATTN_DH, IDX_HEADS * IDX_DH, IDX_DH, IDX_HEADS)
ODD_IN = sum(ODD_SPLITS)
ATTN_WIDTH = ATTN_HEADS * ATTN_DH

kernel_name = 'hybrid_mlstm_gla_dsa_moe_deepnorm'

def split_cols(y, sizes):
    cuts = [int(c) for c in np.cumsum(sizes)[:-1]]
    return jnp.split(y, cuts, axis=-1)

def layer_norm(x, gain, bias):
    xf = x.astype(jnp.float32)
    mu = jnp.mean(xf, axis=-1, keepdims=True)
    var = jnp.mean(jnp.square(xf - mu), axis=-1, keepdims=True)
    y = (xf - mu) * lax.rsqrt(var + LN_EPS) * gain.astype(jnp.float32) + bias.astype(jnp.float32)
    return y.astype(x.dtype)

def head_rms_norm(h, gain):
    hn = h * lax.rsqrt(jnp.mean(jnp.square(h), axis=-1, keepdims=True) + HEAD_NORM_EPS)
    return hn.reshape(h.shape[0], h.shape[1], -1) * gain.astype(jnp.float32)

def causal_depthwise_conv(x, w):
    c = x.shape[-1]
    return lax.conv_general_dilated(x, w[:, None, :].astype(x.dtype), window_strides=(1,), padding=[(w.shape[0] - 1, 0)], dimension_numbers=('NWC', 'WIO', 'NWC'), feature_group_count=c)

def partial_rotary(x, positions, rot_dim):
    half = rot_dim // 2
    inv_freq = 1.0 / (ROPE_THETA ** (jnp.arange(half, dtype=jnp.float32) / half))
    ang = positions.astype(jnp.float32)[:, :, None, None] * inv_freq
    cos, sin = jnp.cos(ang), jnp.sin(ang)
    xr = x[..., :rot_dim].astype(jnp.float32)
    x1, x2 = xr[..., :half], xr[..., half:]
    rot = jnp.concatenate([x1 * cos - x2 * sin, x2 * cos + x1 * sin], axis=-1)
    return jnp.concatenate([rot.astype(x.dtype), x[..., rot_dim:]], axis=-1)

def causal_chunk_mask():
    pos = jnp.arange(CHUNK)
    return pos[:, None] >= pos[None, :]

def mlstm_chunked(q, k, v, i_pre, f_pre):
    f32 = jnp.float32
    bsz, t, h, dk = q.shape
    dv = v.shape[-1]
    nc = t // CHUNK
    q = q.astype(f32).reshape(bsz, nc, CHUNK, h, dk)
    k = (k.astype(f32) * dk ** -0.5).reshape(bsz, nc, CHUNK, h, dk)
    v = v.astype(f32).reshape(bsz, nc, CHUNK, h, dv)
    ig = i_pre.astype(f32).reshape(bsz, nc, CHUNK, h)
    lf = jax.nn.log_sigmoid(f_pre.astype(f32)).reshape(bsz, nc, CHUNK, h)
    b = jnp.cumsum(lf, axis=2)
    b_last = b[:, :, -1]
    a = b_last[:, :, None] - b + ig
    m_loc = jnp.max(a, axis=2)
    wk = jnp.exp(a - m_loc[:, :, None])
    c_loc = jnp.einsum('bnjh,bnjhd,bnjhe->bnhde', wk, k, v)
    n_loc = jnp.einsum('bnjh,bnjhd->bnhd', wk, k)

    def step(carry, inp):
        c, n, m = carry
        g, cl, nl, ml = inp
        m_new = jnp.maximum(g + m, ml)
        s_old = jnp.exp(g + m - m_new)
        s_loc = jnp.exp(ml - m_new)
        c_new = s_old[..., None, None] * c + s_loc[..., None, None] * cl
        n_new = s_old[..., None] * n + s_loc[..., None] * nl
        return (c_new, n_new, m_new), (c, n, m)

    init = (jnp.zeros((bsz, h, dk, dv), f32), jnp.zeros((bsz, h, dk), f32), jnp.zeros((bsz, h), f32))
    xs = (jnp.moveaxis(b_last, 1, 0), jnp.moveaxis(c_loc, 1, 0), jnp.moveaxis(n_loc, 1, 0), jnp.moveaxis(m_loc, 1, 0))
    _, (c_prev, n_prev, m_prev) = lax.scan(step, init, xs)
    c_prev = jnp.moveaxis(c_prev, 0, 1)
    n_prev = jnp.moveaxis(n_prev, 0, 1)
    m_prev = jnp.moveaxis(m_prev, 0, 1)
    d_log = b[:, :, :, None, :] - b[:, :, None, :, :] + ig[:, :, None, :, :]
    d_log = jnp.where(causal_chunk_mask()[None, None, :, :, None], d_log, -jnp.inf)
    inter = b + m_prev[:, :, None]
    m_q = jnp.maximum(inter, jnp.max(d_log, axis=3))
    w_ij = jnp.einsum('bnihd,bnjhd->bnijh', q, k) * jnp.exp(d_log - m_q[:, :, :, None])
    s_int = jnp.exp(inter - m_q)
    num = jnp.einsum('bnijh,bnjhe->bnihe', w_ij, v) + s_int[..., None] * jnp.einsum('bnihd,bnhde->bnihe', q, c_prev)
    den = jnp.sum(w_ij, axis=3) + s_int * jnp.einsum('bnihd,bnhd->bnih', q, n_prev)
    out = num / jnp.maximum(jnp.abs(den), jnp.exp(-m_q))[..., None]
    return out.reshape(bsz, t, h, dv)

def gla_chunked(q, k, v, log_a):
    f32 = jnp.float32
    bsz, t, h, dk = q.shape
    dv = v.shape[-1]
    nc = t // CHUNK
    q = (q.astype(f32) * dk ** -0.5).reshape(bsz, nc, CHUNK, h, dk)
    k = k.astype(f32).reshape(bsz, nc, CHUNK, h, dk)
    v = v.astype(f32).reshape(bsz, nc, CHUNK, h, dv)
    la = jnp.cumsum(log_a.astype(f32).reshape(bsz, nc, CHUNK, h, dk), axis=2)
    la_last = la[:, :, -1]
    q_dec = q * jnp.exp(la)
    k_dec = k * jnp.exp(-la)
    k_end = k * jnp.exp(la_last[:, :, None] - la)
    s_loc = jnp.einsum('bnjhd,bnjhe->bnhde', k_end, v)

    def step(s, inp):
        decay, sl = inp
        return jnp.exp(decay)[..., None] * s + sl, s

    _, s_prev = lax.scan(step, jnp.zeros((bsz, h, dk, dv), f32), (jnp.moveaxis(la_last, 1, 0), jnp.moveaxis(s_loc, 1, 0)))
    s_prev = jnp.moveaxis(s_prev, 0, 1)
    attn = jnp.einsum('bnihd,bnjhd->bnijh', q_dec, k_dec)
    attn = jnp.where(causal_chunk_mask()[None, None, :, :, None], attn, 0.0)
    out = jnp.einsum('bnijh,bnjhe->bnihe', attn, v) + jnp.einsum('bnihd,bnhde->bnihe', q_dec, s_prev)
    return out.reshape(bsz, t, h, dv)

def ab_mixer(x, w_in, conv_w, igate_b, fgate_b, gla_w2, gla_b, mlstm_norm_g, gla_norm_g, w_out):
    f32 = jnp.float32
    bsz, t, _ = x.shape
    mq, mk, mv, mi, mf, mo, gq, gk, gv, glr, gr = split_cols(x @ w_in, EVEN_SPLITS)
    qk = jax.nn.silu(causal_depthwise_conv(jnp.concatenate([mq, mk], axis=-1), conv_w))
    mq, mk = jnp.split(qk, 2, axis=-1)
    hm = mlstm_chunked(mq.reshape(bsz, t, MLSTM_HEADS, MLSTM_DK), mk.reshape(bsz, t, MLSTM_HEADS, MLSTM_DK), mv.reshape(bsz, t, MLSTM_HEADS, MLSTM_DV), mi + igate_b, mf + fgate_b)
    hm = head_rms_norm(hm, mlstm_norm_g) * jax.nn.sigmoid(mo.astype(f32))
    log_a = jax.nn.log_sigmoid((glr @ gla_w2 + gla_b).astype(f32)) / GLA_GATE_TAU
    hg = gla_chunked(gq.reshape(bsz, t, GLA_HEADS, GLA_DK), gk.reshape(bsz, t, GLA_HEADS, GLA_DK), gv.reshape(bsz, t, GLA_HEADS, GLA_DV), log_a.reshape(bsz, t, GLA_HEADS, GLA_DK))
    hg = head_rms_norm(hg, gla_norm_g) * jax.nn.silu(gr.astype(f32))
    return jnp.concatenate([hm, hg], axis=-1).astype(x.dtype) @ w_out

def dsa_mixer(x, positions, w_in, w_out):
    f32 = jnp.float32
    bsz, t, _ = x.shape
    q, k, v, qi, ki, wi = split_cols(x @ w_in, ODD_SPLITS)
    q = partial_rotary(q.reshape(bsz, t, ATTN_HEADS, ATTN_DH), positions, ROPE_DIM).astype(f32)
    k = partial_rotary(k.reshape(bsz, t, ATTN_KV_HEADS, ATTN_DH), positions, ROPE_DIM).astype(f32)
    v = v.reshape(bsz, t, ATTN_KV_HEADS, ATTN_DH).astype(f32)
    qi = partial_rotary(qi.reshape(bsz, t, IDX_HEADS, IDX_DH), positions, IDX_ROPE_DIM).astype(f32)
    ki = partial_rotary(ki.reshape(bsz, t, 1, IDX_DH), positions, IDX_ROPE_DIM)[:, :, 0].astype(f32)
    wi = wi.astype(f32) * (IDX_HEADS ** -0.5 * IDX_DH ** -0.5)
    top_k = min(INDEX_TOPK, t // 4)
    n_blk = t // Q_BLOCK
    key_pos = jnp.arange(t)

    def to_blocks(a):
        return jnp.moveaxis(a.reshape(bsz, n_blk, Q_BLOCK, *a.shape[2:]), 1, 0)

    def block(inp):
        qb, qib, wib, qpos = inp
        idx_logits = jnp.einsum('bqhd,bsd->bqhs', qib, ki)
        score = jnp.einsum('bqhs,bqh->bqs', jax.nn.relu(idx_logits), wib)
        score = jnp.where((key_pos[None, :] <= qpos[:, None])[None], score, -jnp.inf)
        _, sel = lax.top_k(score, top_k)
        valid = sel <= qpos[None, :, None]
        k_sel = jax.vmap(lambda kb, ib: kb[ib])(k, sel)
        v_sel = jax.vmap(lambda vb, ib: vb[ib])(v, sel)
        qg = qb.reshape(bsz, Q_BLOCK, ATTN_KV_HEADS, ATTN_HEADS // ATTN_KV_HEADS, ATTN_DH)
        logits = jnp.einsum('bqgrd,bqkgd->bqgrk', qg, k_sel) * ATTN_DH ** -0.5
        logits = jnp.where(valid[:, :, None, None, :], logits, -jnp.inf)
        p = jax.nn.softmax(logits, axis=-1)
        o = jnp.einsum('bqgrk,bqkgd->bqgrd', p, v_sel)
        return o.reshape(bsz, Q_BLOCK, ATTN_WIDTH)

    out = lax.map(block, (to_blocks(q), to_blocks(qi), to_blocks(wi), key_pos.reshape(n_blk, Q_BLOCK)))
    out = jnp.moveaxis(out, 0, 1).reshape(bsz, t, ATTN_WIDTH)
    return out.astype(x.dtype) @ w_out

def moe_ffn(x, router_w, router_bias, w_gate, w_up, w_down):
    f32 = jnp.float32
    aff = jax.nn.sigmoid(jnp.einsum('btd,de->bte', x.astype(f32), router_w.astype(f32)))
    sel = aff + router_bias.astype(f32)
    grp = sel.reshape(sel.shape[0], sel.shape[1], N_GROUPS, EXPERTS_PER_GROUP)
    grp_score = jnp.sum(lax.top_k(grp, GROUP_SCORE_TOPK)[0], axis=-1)
    g = jnp.argmax(grp_score, axis=-1)
    in_grp = jnp.take_along_axis(grp, g[:, :, None, None], axis=2)[:, :, 0]
    _, loc = lax.top_k(in_grp, TOP_K_EXPERTS)
    e_idx = g[..., None] * EXPERTS_PER_GROUP + loc
    gate = jnp.take_along_axis(aff, e_idx, axis=-1)
    gate = gate / jnp.sum(gate, axis=-1, keepdims=True)
    comb = jnp.sum(jax.nn.one_hot(e_idx, N_EXPERTS, dtype=f32) * gate[..., None], axis=-2)
    hg = jnp.einsum('btd,edf->btef', x, w_gate)
    hu = jnp.einsum('btd,edf->btef', x, w_up)
    h = (jax.nn.silu(hg) * hu).astype(f32) * comb[..., None]
    return jnp.einsum('btef,efd->btd', h.astype(x.dtype), w_down)

def setup_inputs(seed: int = 0) -> dict:
    key = jax.random.key(seed)
    ks = jax.random.split(key, 22)
    f32 = jnp.float32

    def nrm(k, shape, scale):
        return jax.random.normal(k, shape, f32) * scale

    x = nrm(ks[0], (BATCH, SEQ, D_MODEL), 1.0)
    positions = jnp.arange(SEQ, dtype=jnp.int32)[None, :] + jax.random.randint(ks[1], (BATCH, 1), 0, MAX_POS_OFFSET, dtype=jnp.int32)
    ab_w_in = nrm(ks[2], (N_EVEN, D_MODEL, EVEN_IN), D_MODEL ** -0.5)
    ab_conv_w = nrm(ks[3], (N_EVEN, CONV_WIDTH, 2 * MLSTM_HEADS * MLSTM_DK), CONV_WIDTH ** -0.5)
    ab_igate_b = nrm(ks[4], (N_EVEN, MLSTM_HEADS), 0.1)
    ab_fgate_b = jnp.linspace(3.0, 6.0, MLSTM_HEADS, dtype=f32)[None, :] + nrm(ks[5], (N_EVEN, MLSTM_HEADS), 0.1)
    ab_gla_gate_w2 = nrm(ks[6], (N_EVEN, GLA_GATE_RANK, GLA_HEADS * GLA_DK), GLA_GATE_RANK ** -0.5)
    ab_gla_gate_b = nrm(ks[7], (N_EVEN, GLA_HEADS * GLA_DK), 0.1)
    ab_mlstm_norm_g = 1.0 + nrm(ks[8], (N_EVEN, MLSTM_HEADS * MLSTM_DV), 0.02)
    ab_gla_norm_g = 1.0 + nrm(ks[9], (N_EVEN, GLA_HEADS * GLA_DV), 0.02)
    ab_w_out = nrm(ks[10], (N_EVEN, MIX_WIDTH, D_MODEL), MIX_WIDTH ** -0.5 * DEEPNORM_BETA)
    c_w_in = nrm(ks[11], (N_ODD, D_MODEL, ODD_IN), D_MODEL ** -0.5)
    c_w_out = nrm(ks[12], (N_ODD, ATTN_WIDTH, D_MODEL), ATTN_WIDTH ** -0.5 * DEEPNORM_BETA)
    router_w = nrm(ks[13], (D_MODEL, N_EXPERTS), D_MODEL ** -0.5)
    router_bias = nrm(ks[14], (N_EXPERTS,), 0.01)
    moe_w_gate = nrm(ks[15], (DEPTH, N_EXPERTS, D_MODEL, EXPERT_FF), D_MODEL ** -0.5)
    moe_w_up = nrm(ks[16], (DEPTH, N_EXPERTS, D_MODEL, EXPERT_FF), D_MODEL ** -0.5)
    moe_w_down = nrm(ks[17], (DEPTH, N_EXPERTS, EXPERT_FF, D_MODEL), EXPERT_FF ** -0.5 * DEEPNORM_BETA)
    ln_mix_g = 1.0 + nrm(ks[18], (DEPTH, D_MODEL), 0.02)
    ln_mix_b = nrm(ks[19], (DEPTH, D_MODEL), 0.02)
    ln_ffn_g = 1.0 + nrm(ks[20], (DEPTH, D_MODEL), 0.02)
    ln_ffn_b = nrm(ks[21], (DEPTH, D_MODEL), 0.02)
    return {'x': x, 'positions': positions, 'ab_w_in': ab_w_in, 'ab_conv_w': ab_conv_w, 'ab_igate_b': ab_igate_b, 'ab_fgate_b': ab_fgate_b, 'ab_gla_gate_w2': ab_gla_gate_w2, 'ab_gla_gate_b': ab_gla_gate_b, 'ab_mlstm_norm_g': ab_mlstm_norm_g, 'ab_gla_norm_g': ab_gla_norm_g, 'ab_w_out': ab_w_out, 'c_w_in': c_w_in, 'c_w_out': c_w_out, 'router_w': router_w, 'router_bias': router_bias, 'moe_w_gate': moe_w_gate, 'moe_w_up': moe_w_up, 'moe_w_down': moe_w_down, 'ln_mix_g': ln_mix_g, 'ln_mix_b': ln_mix_b, 'ln_ffn_g': ln_ffn_g, 'ln_ffn_b': ln_ffn_b}

def reference(x, positions, ab_w_in, ab_conv_w, ab_igate_b, ab_fgate_b, ab_gla_gate_w2, ab_gla_gate_b, ab_mlstm_norm_g, ab_gla_norm_g, ab_w_out, c_w_in, c_w_out, router_w, router_bias, moe_w_gate, moe_w_up, moe_w_down, ln_mix_g, ln_mix_b, ln_ffn_g, ln_ffn_b):
    h = x
    for layer in range(DEPTH):
        j = layer // 2
        if layer % 2 == 0:
            mix = ab_mixer(h, ab_w_in[j], ab_conv_w[j], ab_igate_b[j], ab_fgate_b[j], ab_gla_gate_w2[j], ab_gla_gate_b[j], ab_mlstm_norm_g[j], ab_gla_norm_g[j], ab_w_out[j])
        else:
            mix = dsa_mixer(h, positions, c_w_in[j], c_w_out[j])
        h = layer_norm(DEEPNORM_ALPHA * h + mix, ln_mix_g[layer], ln_mix_b[layer])
        ffn = moe_ffn(h, router_w, router_bias, moe_w_gate[layer], moe_w_up[layer], moe_w_down[layer])
        h = layer_norm(DEEPNORM_ALPHA * h + ffn, ln_ffn_g[layer], ln_ffn_b[layer])
    return h


_drawn_inputs = setup_inputs


def setup_inputs(seed=0):
    import zlib

    import numpy as np

    out = dict(_drawn_inputs(seed))
    spreads = {}
    factors = {'ab_igate_b': 64.0, 'ab_mlstm_norm_g': 3.256, 'ab_gla_norm_g': 3.027}
    for name, (base, spread) in spreads.items():
        noise = np.random.default_rng([zlib.crc32(name.encode()), seed]).standard_normal(out[name].shape)
        drawn = base * np.exp(spread * noise) if base else spread * noise
        out[name] = __import__('jax').numpy.asarray(drawn.astype(out[name].dtype))
    for name, factor in factors.items():
        out[name] = (out[name] * factor).astype(out[name].dtype)
    return out
```

```python
import math
from contextlib import ExitStack

import numpy as np
import concourse.bass as bass
from concourse import mybir

FP32 = mybir.dt.float32
INT32 = mybir.dt.int32
ALU = mybir.AluOpType
ACT = mybir.ActivationFunctionType
AX = mybir.AxisListType

P = 128
SEQ, D = 256, 2048
TT = SEQ // P
KT = D // P
BANK = 512
SLOT = 4096
NH, DK, DV = 4, 128, 256
CH = 64
RANK = 16
TAPS = 4
AH, KVH, DH = 16, 4, 128
GQ = AH // KVH
IH, IDH = 16, 64
TOPK = min(256, SEQ // 4)
NE, NG, EPG, FF = 16, 4, 4, 512
CAP = 64
MAX_ROUNDS = SEQ // CAP
PAIRS = NE // 2
ALPHA = float((2 * 2) ** 0.25)
LN_EPS, HN_EPS = 1e-5, 1e-6
NEG = -1e30
TAKEN = -3e38

MQ, MK, MV, MI, MO, GQC, GK, GV, GLR, GR = 0, 512, 1024, 2048, 2056, 3080, 3592, 4104, 5128, 5144
AK, AV, QI, KI = 2048, 2560, 3072, 4096

L0_CHUNKS = [MQ, MK, GQC, GK, MV, MV + 512, MO, MO + 512, GV, GV + 512, GR, GR + 512]
L1_CHUNKS = [QI, QI + 512, AK, AV, 0, 512, 1024, 1536]
OUT_CHUNKS = [0, 512, 1024, 1536]


def tile_plan():
    plan = [("xT0", 8, "ADADADAD"), ("rows", 1, "D"), ("gates", 2, "DA")]
    plan += [(f"chunk0_{c}", 4, "DDDD" if c < 2 else "AAAA") for c in range(4)]
    plan += [("decay", 2, "DD"), ("gcols", 1, "D")]
    plan += [("chunk0_4", 2, "AA"), ("chunk0_5", 2, "AA"), ("chunk0_6", 2, "AA"), ("mS0", 2, "DD")]
    plan += [("chunk0_7", 2, "AA"), ("mO0", 2, "DD"), ("mS1", 2, "DD")]
    plan += [("chunk0_8", 2, "AA"), ("mO1", 2, "DD"), ("mS2", 2, "DD")]
    plan += [("chunk0_9", 2, "AA"), ("mO2", 2, "DD"), ("mS3", 2, "DD"), ("kend", 2, "AA")]
    plan += [("chunk0_10", 2, "AA"), ("mO3", 2, "DD"), ("gattn", 2, "DD"), ("gstate", 6, "DDDDDD")]
    plan += [("chunk0_11", 2, "AA"), ("gO", 4, "AAAA"), ("mixT0", 8, "ADADADAD"), ("out0", 8, "D" * 8)]
    plan += [("moeT0", 8, "ADADADAD"), ("route0", 1, "D"), ("pos0", 1, "D")]
    plan += [("xT1", 8, "ADADADAD"), ("small1", 1, "D")]
    plan += [(f"chunk1_{c}", 2, "AA") for c in range(8)]
    plan += [("qiT", 9, "ADADADADA"), ("qkT", 10, "ADADADADAD"), ("index", 12, "D" * 12)]
    for tt in range(TT):
        for g in range(KVH):
            n = 1 if tt == 0 else 2
            plan += [(f"S{tt}_{g}", n, "D" * n), (f"PT{tt}_{g}", n, "A" * n), (f"O{tt}_{g}", 1, "A")]
    plan += [("out1", 8, "D" * 8), ("moeT1", 8, "ADADADAD"), ("route1", 1, "D"), ("pos1", 1, "D")]
    return plan


def psum_order():
    head, tail, scores, rest = [], [], [], []
    groups = {}
    for stage in tile_plan():
        name = stage[0]
        if name[0] in "SPO" and "_" in name:
            groups[name] = stage
        elif not groups:
            head.append(stage)
        else:
            tail.append(stage)
    keys = [f"{tt}_{g}" for tt in range(TT) for g in range(KVH)]
    for n, key in enumerate(keys):
        if n == 0:
            rest.append(groups["S" + key])
        if n + 1 < len(keys):
            rest.append(groups["S" + keys[n + 1]])
        rest += [groups["PT" + key], groups["O" + key]]
    return head + rest + tail


def program(nc, a, out):
    first, drained_by, n = {}, "", 0
    for stage, count, engines in psum_order():
        assert len(engines) == count, stage
        first[stage] = n
        drained_by += engines
        n += count

    ctx = ExitStack()
    with ctx:
        def sbuf(name, shape, dt=FP32):
            return ctx.enter_context(nc.sbuf_tensor(name, shape, dt))

        def sem(name):
            return ctx.enter_context(nc.semaphore(name))

        h = sbuf("h", [P, TT, D])
        hT = sbuf("hT", [P, KT, SEQ])
        ring = sbuf("ring", [P, 3 * SLOT])
        arena = sbuf("arena", [P, 18432])
        arena2 = sbuf("arena2", [P, 3 * SLOT])
        ident = sbuf("ident", [P, P])
        maskT = sbuf("maskT", [P, SEQ])
        maskN = sbuf("maskN", [P, SEQ])
        before = sbuf("before", [P, P])
        ones = sbuf("ones", [P, P])
        slots64 = sbuf("slots64", [P, CAP])
        router_w = sbuf("router_w", [P, KT, NE])
        router_b = sbuf("router_b", [P, NE])
        mhalf = sbuf("mhalf", [P, 16])
        stats = sbuf("stats", [P, TT, 4, 6])
        mean_var = sbuf("mean_var", [P, TT, 2])
        var_eps = sbuf("var_eps", [P, TT])
        rstd = sbuf("rstd", [P, TT])
        rounds_f = sbuf("rounds_f", [P, 4])
        rounds_i = sbuf("rounds_i", [P, 1], INT32)
        pos_int = sbuf("pos_int", [P, TT], INT32)
        small_rows = sbuf("small_rows", [TAPS * 8 + 4, P])
        small_cols = sbuf("small_cols", [P, TAPS * 8 + 4])
        gate_bias = sbuf("gate_bias", [NH, 2])

        def slot(s):
            return ring[:, s * SLOT:(s + 1) * SLOT] if s < 3 else arena2[:, (s - 3) * SLOT:(s - 2) * SLOT]

        def carve(tensor, start, shape):
            size = 1
            for x in shape:
                size *= x
            assert start + size <= tensor.shape[1], (start, shape)
            v = tensor[:, start:start + size]
            if len(shape) == 2:
                v = v.rearrange("p (a b) -> p a b", b=shape[1])
            if len(shape) == 3:
                v = v.rearrange("p (a b c) -> p a b c", b=shape[1], c=shape[2])
            return v, start + size

        V, o = carve(arena, 0, [TT, 2 * NH, DV + 1])
        mix, o = carve(arena, o, [TT, D])
        QKT, o = carve(arena, o, [16, SEQ])
        norm_g, o = carve(arena, o, [D])
        w_small0, o = carve(arena, o, [KT, 24])
        w2, o = carve(arena, o, [NH * DK])
        pick, o = carve(arena, o, [NH, P])
        hn, o = carve(arena, o, [TT * NH, DV])
        ssq, o = carve(arena, o, [2 * TT * NH])
        hn_r, o = carve(arena, o, [2 * TT * NH])
        ssq_m, o = carve(arena, o, [2 * TT * NH])
        gcol, o = carve(arena, o, [4, NH])
        la_last, o = carve(arena, o, [NH * 4])
        decay, o = carve(arena, o, [NH * 4])
        den_r, o = carve(arena, o, [4])
        la, o = carve(arena2, 0, [NH * SEQ])
        t1, o = carve(arena2, o, [NH * SEQ])
        t2, o = carve(arena2, o, [NH * SEQ])
        t3, o = carve(arena2, o, [NH * SEQ])
        resets, o = carve(arena2, o, [NH * SEQ])
        kz_at = o
        kz, o = carve(arena2, o, [TT * NH, 2, DK])
        attnT, o = carve(arena2, o, [TT * NH, P])
        s_at = o
        state, o = carve(arena2, o, [3, NH, DV])
        Dl, k = carve(arena2, kz_at, [2, 384])
        W, k = carve(arena2, k, [2, 384])
        row = {}
        k = s_at
        for name in ("xf", "ab", "lf", "b", "ig", "g", "M", "nM", "m", "e", "one"):
            row[name], k = carve(arena2, k, [SEQ])
            row[name] = row[name][0:NH, :]
        chunk_mask = carve(arena2, o, [P])[0].bitcast(INT32)
        cmf, _ = carve(arena2, o + P, [P])

        ln_gb, o = carve(arena, 0, [2, D])
        acc, o = carve(arena, o, [TT, D])
        xc_at = o
        xcT, o = carve(arena, o, [KT, 2 * CAP])
        y_sb, o = carve(arena, o, [2 * BANK])
        pick_p, o = carve(arena, o, [TT, 2 * CAP])
        pick_w, o = carve(arena, o, [2, TT, 3 * CAP])
        pw_T, o = carve(arena, o, [2, TT, P])
        silu_g, o = carve(arena, o, [DV])
        h_e, o = carve(arena, o, [DV])
        hT_e, o = carve(arena, o, [2, P])
        pos_r, o = carve(arena, o, [TT, MAX_ROUNDS * NE])
        comb_r, o = carve(arena, o, [TT, MAX_ROUNDS * NE])
        aff, k = carve(arena, xc_at, [TT, NE])
        sel, k = carve(arena, k, [TT, NE])
        rank, k = carve(arena, k, [TT, NE])
        cmp, k = carve(arena, k, [TT, NE])
        cmp2, k = carve(arena, k, [TT, NE])
        pairs6, k = carve(arena, k, [TT * NG, 6])
        gsc, k = carve(arena, k, [TT, NG])
        grank, k = carve(arena, k, [TT, NG])
        chosen, k = carve(arena, k, [TT, NE])
        csum, k = carve(arena, k, [TT, 1])
        crec, k = carve(arena, k, [TT, 1])

        QN, o = carve(arena, 0, [TT, (AH + KVH), DH])
        QIN, o = carve(arena, o, [TT, IH + 1, IDH])
        VN, o = carve(arena, o, [TT, KVH, DH])
        qT, o = carve(arena, o, [AH + KVH, SEQ])
        score, o = carve(arena, o, [TT, SEQ])
        work, o = carve(arena, o, [TT, SEQ])
        wi, o = carve(arena, o, [TT, IH])
        angles, o = carve(arena, o, [TT, 24])
        freq, o = carve(arena, o, [24])
        cosv, o = carve(arena, o, [TT, 24])
        sinv, o = carve(arena, o, [TT, 24])
        kf, o = carve(arena, o, [2, TT * 24])
        pos_f, o = carve(arena, o, [TT])
        top8, o = carve(arena, o, [TT, 8])
        mx, o = carve(arena, o, [2, 3 * GQ])
        qiT, o = carve(arena2, 0, [IH + 1, SEQ])
        w_small1, k = carve(arena2, o, [KT, 80])
        R, o2 = carve(arena2, o, [IH, SEQ])
        rope_t, k = carve(arena2, o, [4, TT * (AH + KVH) * 16])
        X = [carve(arena2, 4352 + 1024 * i, [GQ, SEQ])[0] for i in range(2)]
        PT = [carve(arena2, 6400 + 1024 * i, [TT, GQ * P])[0] for i in range(2)]

        ps = [ctx.enter_context(nc.psum_tensor(f"ps{i}", [P, BANK], FP32)) for i in range(8)]

        small_loaded = sem("small_loaded")
        x_loaded = sem("x_loaded")
        ln_loaded = sem("ln_loaded")
        small1_loaded = sem("small1_loaded")
        out_stored = sem("out_stored")
        consts_ready = sem("consts_ready")
        pool_step = sem("pool_step")
        psum_full = sem("psum_full")
        drained = {"A": sem("drained_by_act"), "D": sem("drained_by_dve")}
        half_used = [sem("half_used_0"), sem("half_used_1")]
        unit_loaded = [[sem(f"unit_loaded_{lay}_{s}") for s in range(3)] for lay in range(2)]
        dve = sem("dve_step")
        act_s = sem("act_step")
        h_ready = sem("h_ready")
        var_ready = sem("var_ready")
        rstd_ready = sem("rstd_ready")
        conv_done = sem("conv_done")
        qk_silu = sem("qk_silu")
        lf_abs = sem("lf_abs")
        lf_log = sem("lf_log")
        rows_done = sem("rows_done")
        e_done = sem("e_done")
        cols_done = sem("cols_done")
        gla_x = sem("gla_x")
        gla_log = sem("gla_log")
        la_done = sem("la_done")
        gla_exp = sem("gla_exp")
        qdec_done = sem("qdec_done")
        kend_done = sem("kend_done")
        kz_zero = sem("kz_zero")
        D_ready = sem("D_ready")
        E_ready = sem("E_ready")
        W_ready = sem("W_ready")
        hn_ready = sem("hn_ready")
        ssq_ready = sem("ssq_ready")
        ssq_scaled = sem("ssq_scaled")
        hr_ready = sem("hr_ready")
        gates_done = sem("gates_done")
        attn_ready = sem("attn_ready")
        state_ready = sem("state_ready")
        mlstm_mixed = sem("mlstm_mixed")
        mix_ready = sem("mix_ready")
        aff_ready = sem("aff_ready")
        logits_ready = sem("logits_ready")
        mask_ready = sem("mask_ready")
        routed = sem("routed")
        trig_in = sem("trig_in")
        trig_out = sem("trig_out")
        roped = sem("roped")
        scored = sem("scored")
        X_ready = sem("X_ready")
        exp_ready = sem("exp_ready")
        P_ready = sem("P_ready")
        mixer1_done = sem("mixer1_done")
        M = []
        for lay in range(2):
            s = {name: sem(f"{name}_{lay}") for name in (
                "gate0_used", "gate_full", "up0_used", "up_full", "down0_used", "y_full", "silu_ready",
                "h_ready", "hT_full", "hT_ready", "xc_full", "xc_drained", "y_ready", "sc_full",
                "sc_drained", "pick_ready", "pw_ready")}
            s["loaded"] = [sem(f"expert_unit_loaded_{lay}_{i}") for i in range(6)]
            M.append(s)
        block = ctx.enter_context(nc.Block())

        def filled(stage, i=0):
            return first[stage] + i + 1

        def tile(stage, i=0):
            return ps[(first[stage] + i) % 8]

        def drained_before(eng, stage, i=0):
            t = first[stage] + i - 8
            if t >= 0:
                who = drained_by[t]
                eng.wait_ge(drained[who], drained_by[:t + 1].count(who))

        def all_drained(eng, stage):
            for who in "AD":
                eng.wait_ge(drained[who], drained_by[:first[stage]].count(who))

        w_in = [a["ab_w_in"][0], a["c_w_in"][0]]
        w_out = [a["ab_w_out"][0], a["c_w_out"][0]]
        chunks = [L0_CHUNKS, L1_CHUNKS]

        def chunk_source(lay, c, u):
            n_in = len(chunks[lay])
            w, col = (w_in[lay], chunks[lay][c]) if c < n_in else (w_out[lay], OUT_CHUNKS[c - n_in])
            return w.rearrange("(k p) n -> p k n", p=P)[:, 8 * u:8 * u + 8, col:col + 512]

        def chunk_stage(lay, c):
            n_in = len(chunks[lay])
            if c < n_in:
                return f"chunk{lay}_{c}", (3 if lay == 0 and c < 4 else 1)
            return f"out{lay}", 2 * (c - n_in) + 1

        gate_w = a["moe_w_gate"].rearrange("l e (p k) n -> l e p (k n)", k=KT)
        up_w = a["moe_w_up"].rearrange("l e (p k) n -> l e p (k n)", k=KT)
        down_w = a["moe_w_down"].rearrange("l e (g p j) n -> l e g p (j n)", g=2, j=2)

        @block.sync
        def _(sp):
            xr = a["x"][0].rearrange("(t p) d -> p t d", p=P)
            for tt in range(TT):
                sp.dma_start(h[:, tt, :], xr[:, tt, :]).then_inc(x_loaded, 16)
            with nc.allow_non_contiguous_dma(reason="columns of the gates, once"):
                wr = w_in[0].rearrange("(k p) n -> p k n", p=P)
                sp.dma_start(w_small0[:, :, 0:8], wr[:, :, MI:MI + 8]).then_inc(small_loaded, 16)
                sp.dma_start(w_small0[:, :, 8:24], wr[:, :, GLR:GLR + RANK]).then_inc(small_loaded, 16)
                sp.dma_start(gate_bias[:, 0:1], a["ab_igate_b"].rearrange("a h -> h a")).then_inc(small_loaded, 16)
                sp.dma_start(gate_bias[:, 1:2], a["ab_fgate_b"].rearrange("a h -> h a")).then_inc(small_loaded, 16)
                sp.dma_start(pos_int[:, :], a["positions"].rearrange("a (t p) -> p (a t)", p=P)).then_inc(small_loaded, 16)
            sp.dma_start(small_rows[0:TAPS * 8, :], a["ab_conv_w"].rearrange("a t (j p) -> (a t j) p", p=P)).then_inc(small_loaded, 16)
            sp.dma_start(small_rows[TAPS * 8:TAPS * 8 + 4, :], a["ab_gla_gate_b"].rearrange("a (j p) -> (a j) p", p=P)).then_inc(small_loaded, 16)
            sp.dma_start(w2[0:RANK, :], a["ab_gla_gate_w2"][0]).then_inc(small_loaded, 16)
            sp.dma_start(router_w[:, :, :], a["router_w"].rearrange("(k p) e -> p k e", p=P)).then_inc(small_loaded, 16)
            sp.dma_start(router_b[:, :], a["router_bias"].partition_broadcast(P)).then_inc(small_loaded, 16)
            sp.dma_start(norm_g[:, 0:1024], a["ab_mlstm_norm_g"][0].partition_broadcast(P)).then_inc(small_loaded, 16)
            sp.dma_start(norm_g[:, 1024:2048], a["ab_gla_norm_g"][0].partition_broadcast(P)).then_inc(small_loaded, 16)

            def load_chunk(lay, c):
                for u in range(2):
                    n = 2 * c + u
                    if n >= 3:
                        pc, pu = (n - 3) // 2, (n - 3) % 2
                        if pu == 0:
                            sp.wait_ge(half_used[lay], pc + 1)
                        else:
                            sp.wait_ge(psum_full, filled(*chunk_stage(lay, pc)))
                    elif lay == 1:
                        wait_last_expert(n)
                    sp.dma_start(slot(n % 3).rearrange("p (k n) -> p k n", k=8), chunk_source(lay, c, u))\
                      .then_inc(unit_loaded[lay][n % 3], 16)

            order = [3, 4, 5, 0, 1, 2]
            used = ["gate0_used", "gate_full", "up0_used", "up_full", "down0_used", "y_full"]

            def expert_source(lay, e, i):
                if i < 4:
                    w = gate_w if i < 2 else up_w
                    v = w[lay, e] if isinstance(e, int) else w[lay, bass.ds(e, 1)][0]
                    return v[:, (i % 2) * SLOT:(i % 2 + 1) * SLOT]
                v = down_w[lay, e] if isinstance(e, int) else down_w[lay, bass.ds(e, 1)][0]
                return v[i - 4]

            def load_expert(lay, e, x, units):
                for i in units:
                    if not (isinstance(x, int) and x == 0):
                        sp.wait_ge(M[lay][used[i]], x)
                    sp.dma_start(slot(order[i]), expert_source(lay, e, i)).then_inc(M[lay]["loaded"][i], 16)

            def wait_last_expert(s):
                sp.wait_ge(M[0][used[s + 3]], NE * n_rounds[0])

            n_rounds = [None, None]
            for lay in range(2):
                nch = len(chunks[lay]) + 4
                for c in range(nch - 3):
                    load_chunk(lay, c)
                    if lay == 1 and c == 0:
                        sp.wait_ge(M[0]["up_full"], NE * n_rounds[0])
                        with nc.allow_non_contiguous_dma(reason="80 columns, once"):
                            sp.dma_start(w_small1[:, :, :], w_in[1].rearrange("(k p) n -> p k n", p=P)[:, :, KI:KI + 80])\
                              .then_inc(small1_loaded, 16)
                sp.wait_ge(mix_ready if lay == 0 else mixer1_done, 1)
                load_expert(lay, 0, 0, [0, 1, 2])
                for c in range(nch - 3, nch):
                    load_chunk(lay, c)
                for i in range(3, 6):
                    sp.wait_ge(psum_full, filled(f"out{lay}", 7))
                load_expert(lay, 0, 0, [3, 4, 5])
                with sp.Fori(1, NE) as e:
                    load_expert(lay, e, e, range(6))
                sp.wait_ge(routed, lay + 1)
                n_rounds[lay] = sp.value_load(rounds_i[0:1, 0:1], min_val=0, max_val=MAX_ROUNDS - 1) + 1
                with sp.If(n_rounds[lay] > 1):
                    with sp.Fori(1, n_rounds[lay]) as r:
                        with sp.Fori(0, NE) as e:
                            load_expert(lay, e, r * NE + e, range(6))
            for tt in range(TT):
                sp.wait_ge(h_ready, 3 * TT + tt + 1)
                sp.dma_start(out[0].rearrange("(t p) d -> p t d", p=P)[:, tt, :], h[:, tt, :]).then_inc(out_stored, 16)
            sp.wait_ge(out_stored, 16 * TT)

        @block.gpsimd
        def _(pool):
            step = [0]

            def link(ins):
                step[0] += 1
                ins.then_inc(pool_step, 1)
                pool.wait_ge(pool_step, step[0])

            pool.memset(ident[:, :], 0.0)
            pool.memset(maskT[:, :], 0.0)
            pool.memset(maskN[:, :], 0.0)
            pool.memset(before[:, :], 0.0)
            pool.memset(ones[:, :], 1.0)
            pool.memset(mhalf[:, :], -0.5)
            pool.memset(pick[0:NH, :, :], 0.0)
            pool.memset(resets[:, :], 1.0)
            pool.memset(V[:, :, :, DV:DV + 1], 1.0)
            link(pool.memset(cmf[:, :], 0.0))
            pool.affine_select(out=ident[:, :], in_=ident[:, :], compare_op=ALU.not_equal, fill=1.0, base=0,
                               pattern=[[-1, P]], channel_multiplier=1)
            pool.affine_select(out=maskT[:, 0:P], in_=maskT[:, 0:P], compare_op=ALU.is_ge, fill=NEG, base=0,
                               pattern=[[1, P]], channel_multiplier=-1)
            pool.affine_select(out=maskN[:, P:2 * P], in_=maskN[:, P:2 * P], compare_op=ALU.is_ge, fill=NEG, base=0,
                               pattern=[[-1, P]], channel_multiplier=1)
            pool.affine_select(out=before[:, :], in_=before[:, :], compare_op=ALU.is_ge, fill=1.0, base=0,
                               pattern=[[-1, P]], channel_multiplier=1)
            pool.affine_select(out=pick[0:NH, :, :], in_=pick[0:NH, :, :], compare_op=ALU.not_equal, fill=1.0, base=0,
                               pattern=[[-1, NH], [0, P]], channel_multiplier=1)
            link(pool.memset(resets[:, :].rearrange("p (a b) -> p a b", b=CH)[:, :, 0:1], 0.0))
            link(pool.affine_select(out=cmf[:, :], in_=cmf[:, :], compare_op=ALU.is_gt, fill=1.0, base=0,
                                    pattern=[[-1, P]], channel_multiplier=1))
            link(pool.memset(cmf[0:CH, CH:P], 0.0))
            link(pool.tensor_copy(chunk_mask, cmf[:, :]))
            link(pool.iota(slots64[:, :], pattern=[[1, CAP]], base=0, channel_multiplier=0,
                           allow_small_or_imprecise_dtypes=True))
            pool.memset(mhalf[:, 0:1], -0.5).then_inc(consts_ready, 1)

            def load_ln(n, g, b):
                pool.dma_start(ln_gb[:, 0, :], g.partition_broadcast(P)).then_inc(ln_loaded, 16)
                pool.dma_start(ln_gb[:, 1, :], b.partition_broadcast(P)).then_inc(ln_loaded, 16)

            def rstd_step(n):
                pool.wait_ge(var_ready, n + 1)
                pool.tensor_tensor(rstd[:, :], var_eps[:, :], mhalf[:, 0:TT], ALU.pow).then_inc(rstd_ready, 1)

            for lay in range(2):
                if lay == 0:
                    for br in range(2):
                        pool.wait_ge(ssq_scaled, br + 1)
                        sl = slice(br * TT * NH, (br + 1) * TT * NH)
                        pool.tensor_tensor(hn_r[:, sl], ssq_m[:, sl], mhalf[:, 0:TT * NH], ALU.pow).then_inc(hr_ready, 1)
                    pool.wait_ge(mix_ready, 1)
                else:
                    pool.wait_ge(mixer1_done, 1)
                load_ln(2 * lay, a["ln_mix_g"][lay], a["ln_mix_b"][lay])
                rstd_step(2 * lay)
                pool.wait_ge(h_ready, TT * (2 * lay + 1))
                load_ln(2 * lay + 1, a["ln_ffn_g"][lay], a["ln_ffn_b"][lay])
                rstd_step(2 * lay + 1)

        @block.tensor
        def _(pe):
            def transposes(stage, i, sources, identity=None):
                drained_before(pe, stage, i)
                t = tile(stage, i)
                for n, src in enumerate(sources):
                    k = src.shape[0]
                    m = src.shape[1]
                    last = nc.tensor.transpose(t[0:m, n * P:n * P + k], src, ident[0:k, 0:k])
                last.then_inc(psum_full, 1)

            def transpose_hidden(stage, src):
                for i in range(8):
                    transposes(stage, i, [src[:, tt, (2 * i + k) * P:(2 * i + k + 1) * P] for k in range(2) for tt in range(TT)])

            def wait_hT(stage):
                t = first[stage] + 7
                for who in "AD":
                    pe.wait_ge(drained[who], drained_by[:t + 1].count(who))

            def wait_unit(lay, n):
                pe.wait_ge(unit_loaded[lay][n % 3], 16 * (n // 3 + 1))

            def chunk_transposed(lay, c):
                stage = f"chunk{lay}_{c}"
                for u in range(2):
                    wait_unit(lay, 2 * c + u)
                    w = slot((2 * c + u) % 3).rearrange("p (k n) -> p k n", k=8)
                    for j in range(4):
                        if u == 0:
                            drained_before(pe, stage, j)
                        for k in range(8):
                            last = nc.tensor.matmul(tile(stage, j)[:, 0:SEQ], w[:, k, j * P:(j + 1) * P], hT[:, 8 * u + k, :],
                                                    start=(u + k == 0), stop=(u == 1 and k == 7))
                        if u == 1:
                            last.then_inc(psum_full, 1)
                    if u == 0:
                        last.then_inc(half_used[lay], 1)

            def chunk_natural(lay, c):
                stage, lt = chunk_stage(lay, c)
                for u in range(2):
                    wait_unit(lay, 2 * c + u)
                    w = slot((2 * c + u) % 3).rearrange("p (k n) -> p k n", k=8)
                    for tt in range(TT):
                        i = lt - 1 + tt
                        if u == 0:
                            drained_before(pe, stage, i)
                        for k in range(8):
                            last = nc.tensor.matmul(tile(stage, i)[:, :], hT[:, 8 * u + k, tt * P:(tt + 1) * P], w[:, k, :],
                                                    start=(u + k == 0), stop=(u == 1 and k == 7))
                        if u == 1:
                            last.then_inc(psum_full, 1)
                    if u == 0:
                        last.then_inc(half_used[lay], 1)

            def mlstm_scores(hd):
                stage = f"mS{hd}"
                drained_before(pe, stage, 0)
                pe.wait_ge(rows_done, 1)
                nc.tensor.matmul(tile(stage, 0)[:, 0:SEQ], pick[0:NH, hd, :], row["nM"], start=True, stop=True).then_inc(psum_full, 1)
                drained_before(pe, stage, 1)
                pe.wait_ge(qk_silu, 8)
                t = tile(stage, 1)
                nc.tensor.matmul(t[:, 0:SEQ], QKT[:, 4 + hd, 0:P], QKT[:, hd, :], start=True, stop=True)
                nc.tensor.matmul(t[:, SEQ:SEQ + P], QKT[:, 4 + hd, P:2 * P], QKT[:, hd, P:2 * P], start=True, stop=True).then_inc(psum_full, 1)

            def mlstm_out(hd):
                stage = f"mO{hd}"
                w = W[:, hd % 2, :]
                pe.wait_ge(W_ready, hd + 1)
                drained_before(pe, stage, 0)
                nc.tensor.matmul(tile(stage, 0)[:, 0:DV + 1], w[:, 0:P], V[:, 0, hd, :], start=True, stop=True).then_inc(psum_full, 1)
                drained_before(pe, stage, 1)
                nc.tensor.matmul(tile(stage, 1)[:, 0:DV + 1], w[:, P:2 * P], V[:, 0, hd, :], start=True, stop=False)
                nc.tensor.matmul(tile(stage, 1)[:, 0:DV + 1], w[:, 2 * P:3 * P], V[:, 1, hd, :], start=False, stop=True).then_inc(psum_full, 1)

            def wait_values(stage):
                t = first[stage] + 1
                pe.wait_ge(drained["A"], drained_by[:t + 1].count("A"))

            pe.wait_ge(consts_ready, 1)
            pe.wait_ge(x_loaded, 16 * TT)
            transpose_hidden("xT0", h)
            pe.wait_ge(small_loaded, 16 * 12)
            transposes("rows", 0, [small_rows[:, :]])
            wait_hT("xT0")
            drained_before(pe, "gates", 0)
            for g in range(2):
                for k in range(KT):
                    last = nc.tensor.matmul(tile("gates", 0)[0:NH, g * SEQ:(g + 1) * SEQ], w_small0[:, k, 4 * g:4 * g + 4],
                                            hT[:, k, :], start=(k == 0), stop=(k == KT - 1))
            last.then_inc(psum_full, 1)
            drained_before(pe, "gates", 1)
            for k in range(KT):
                last = nc.tensor.matmul(tile("gates", 1)[0:RANK, 0:SEQ], w_small0[:, k, 8:24], hT[:, k, :],
                                        start=(k == 0), stop=(k == KT - 1))
            last.then_inc(psum_full, 1)
            for c in range(4):
                chunk_transposed(0, c)
            t = first["gates"] + 1
            pe.wait_ge(drained["A"], drained_by[:t + 1].count("A"))
            for i in range(2):
                drained_before(pe, "decay", i)
                for j in range(2):
                    hd = 2 * i + j
                    last = nc.tensor.matmul(tile("decay", i)[:, j * SEQ:(j + 1) * SEQ], w2[0:RANK, hd * DK:(hd + 1) * DK],
                                            t3[0:RANK, 0:SEQ], start=True, stop=True)
                last.then_inc(psum_full, 1)
            pe.wait_ge(e_done, 1)
            pe.wait_ge(rows_done, 1)
            transposes("gcols", 0, [row["g"][:, 0:P], row["g"][:, P:2 * P], row["e"][:, 0:P], row["e"][:, P:2 * P]])
            chunk_natural(0, 4)
            chunk_natural(0, 5)
            chunk_natural(0, 6)
            mlstm_scores(0)
            for hd in range(1, NH):
                chunk_natural(0, 6 + hd)
                if hd == 1:
                    wait_values("chunk0_5")
                mlstm_out(hd - 1)
                mlstm_scores(hd)
            pe.wait_ge(kend_done, 1)
            for tt in range(TT):
                transposes("kend", tt, [t3[:, hd * SEQ + tt * P:hd * SEQ + (tt + 1) * P] for hd in range(NH)])
            chunk_natural(0, 10)
            mlstm_out(NH - 1)
            pe.wait_ge(qdec_done, 2)
            for tt in range(TT):
                drained_before(pe, "gattn", tt)
                for hd in range(NH):
                    last = nc.tensor.matmul(tile("gattn", tt)[:, hd * P:(hd + 1) * P], QKT[:, 12 + hd, tt * P:(tt + 1) * P],
                                            QKT[:, 8 + hd, tt * P:(tt + 1) * P], start=True, stop=True)
                last.then_inc(psum_full, 1)
            wait_values("chunk0_9")
            t = first["kend"] + 1
            pe.wait_ge(drained["A"], drained_by[:t + 1].count("A"))
            for c in range(3):
                for hp in range(2):
                    i = 2 * c + hp
                    drained_before(pe, "gstate", i)
                    for j in range(2):
                        hd = 2 * hp + j
                        last = nc.tensor.matmul(tile("gstate", i)[:, j * DV:(j + 1) * DV], kz[:, (c // 2) * NH + hd, c % 2, :],
                                                V[:, c // 2, NH + hd, 0:DV], start=True, stop=True)
                    last.then_inc(psum_full, 1)
            chunk_natural(0, 11)
            pe.wait_ge(attn_ready, TT)
            for tt in range(TT):
                pe.wait_ge(state_ready, 6 if tt else 2)
                for hp in range(2):
                    i = 2 * tt + hp
                    drained_before(pe, "gO", i)
                    for j in range(2):
                        hd = 2 * hp + j
                        o_t = tile("gO", i)[:, j * DV:(j + 1) * DV]
                        nc.tensor.matmul(o_t, attnT[:, tt * NH + hd, :], V[:, tt, NH + hd, 0:DV], start=True, stop=False,
                                         skip_group_check=True)
                        for c in ([1] if tt == 0 else [2, 3]):
                            r0 = (c % 2) * CH
                            last = nc.tensor.matmul(tile("gO", i)[r0:r0 + CH, j * DV:(j + 1) * DV],
                                                    QKT[:, 8 + hd, c * CH:(c + 1) * CH], state[:, c - 1, hd, :],
                                                    start=False, stop=True, skip_group_check=True)
                    last.then_inc(psum_full, 1)
            pe.wait_ge(mix_ready, 1)
            transpose_hidden("mixT0", mix)
            wait_hT("mixT0")
            for c in range(12, 16):
                chunk_natural(0, c)

            def experts(lay):
                s = M[lay]
                pe.wait_ge(h_ready, TT * (2 * lay + 1))
                transpose_hidden(f"moeT{lay}", h)
                wait_hT(f"moeT{lay}")
                drained_before(pe, f"route{lay}", 0)
                for tt in range(TT):
                    for k in range(KT):
                        last = nc.tensor.matmul(tile(f"route{lay}")[:, tt * NE:(tt + 1) * NE], hT[:, k, tt * P:(tt + 1) * P],
                                                router_w[:, k, :], start=(k == 0), stop=(k == KT - 1))
                last.then_inc(psum_full, 1)
                pe.wait_ge(mask_ready, lay + 1)
                drained_before(pe, f"pos{lay}", 0)
                t = tile(f"pos{lay}")
                nc.tensor.matmul(t[:, 0:NE], before[:, :], chosen[:, 0, :], start=True, stop=True)
                nc.tensor.matmul(t[:, NE:2 * NE], ones[:, :], chosen[:, 0, :], start=True, stop=False)
                nc.tensor.matmul(t[:, NE:2 * NE], before[:, :], chosen[:, 1, :], start=False, stop=True)
                nc.tensor.matmul(t[:, 2 * NE:3 * NE], ones[:, :], chosen[:, 0, :], start=True, stop=False)
                nc.tensor.matmul(t[:, 2 * NE:3 * NE], ones[:, :], chosen[:, 1, :], start=False, stop=True).then_inc(psum_full, 1)
                pe.wait_ge(routed, lay + 1)
                n_r = pe.value_load(rounds_i[0:1, 0:1], min_val=0, max_val=MAX_ROUNDS - 1) + 1

                def gather(tiles_before, pair):
                    pe.wait_ge(s["pick_ready"], pair + 1)
                    for g in range(4):
                        bank = ps[4 + g % 2]
                        if not (isinstance(tiles_before, int) and tiles_before + g < 2):
                            pe.wait_ge(s["xc_drained"], tiles_before + g - 1)
                        for k in range(4):
                            for tt in range(TT):
                                last = nc.tensor.matmul(bank[:, k * P:(k + 1) * P], h[:, tt, 4 * g + k::KT], pick_p[:, tt, :],
                                                        start=(tt == 0), stop=(tt == TT - 1))
                        last.then_inc(s["xc_full"], 1)

                def scatter_tile(x, t8):
                    c, tt = t8 // 2, t8 % 2
                    if not (isinstance(x, int) and x == 0 and t8 < 2):
                        pe.wait_ge(s["sc_drained"], 8 * x + t8 - 1)
                    nc.tensor.matmul(ps[6 + t8 % 2][:, :], pw_T[:, c // 2, tt, :], y_sb[:, (c % 2) * BANK:(c % 2 + 1) * BANK],
                                     start=True, stop=True).then_inc(s["sc_full"], 1)

                def expert(q, i, is_first, is_last):
                    x = 2 * q + i
                    begun = not (is_first and i == 0)
                    units = [slot(n) for n in (3, 4, 5, 0, 1, 2)]
                    if i == 0:
                        pe.wait_ge(s["xc_drained"], 6 * q + 4)
                    for part in range(4):
                        pe.wait_ge(s["loaded"][part], 16 * (x + 1))
                        w = units[part].rearrange("p (k n) -> p k n", k=8)
                        for k in range(8):
                            kt = 8 * (part % 2) + k
                            for hf in range(2):
                                last = nc.tensor.matmul(ps[part // 2][hf * CAP:(hf + 1) * CAP, 0:DV],
                                                        xcT[:, kt, i * CAP:(i + 1) * CAP], w[:, k, hf * DV:(hf + 1) * DV],
                                                        start=(kt == 0), stop=(kt == KT - 1), skip_group_check=True)
                        last.then_inc(s[("gate0_used", "gate_full", "up0_used", "up_full")[part]], 1)
                    if begun:
                        pe.wait_ge(s["y_ready"], x)
                        pe.wait_ge(s["xc_drained"], (6 * q + 4) if i == 0 else (6 * q + 5))
                        for t8 in range(6):
                            scatter_tile(x - 1, t8)
                    pe.wait_ge(s["h_ready"], x + 1)
                    for j in range(2):
                        last = nc.tensor.transpose(ps[0][:, j * P:(j + 1) * P], h_e[:, j::2], ident[:, :])
                    last.then_inc(s["hT_full"], 1)
                    if begun:
                        for t8 in range(6, 8):
                            scatter_tile(x - 1, t8)
                    pe.wait_ge(s["pw_ready"], x + 1)
                    pe.wait_ge(s["xc_drained"], 6 * q + 3 + i)
                    for ab in range(2):
                        for tt in range(TT):
                            last = nc.tensor.transpose(ps[4 + i][:, (ab * TT + tt) * P:(ab * TT + tt + 1) * P],
                                                       pick_w[:, i, tt, CAP * (1 - ab):CAP * (1 - ab) + P], ident[:, :])
                    last.then_inc(s["xc_full"], 1)
                    if i == 1 and not is_last:
                        gather(6 * q + 6, q + 1)
                    pe.wait_ge(s["hT_ready"], x + 1)
                    if begun:
                        pe.wait_ge(s["y_ready"], x)
                    for hf in range(2):
                        pe.wait_ge(s["loaded"][4 + hf], 16 * (x + 1))
                        w = units[4 + hf].rearrange("p (j n) -> p j n", j=2)
                        for j in range(2):
                            for cc in range(2):
                                for side in range(2):
                                    col = side * 2 * BANK + cc * BANK
                                    last = nc.tensor.matmul(ps[2 + cc][side * CAP:(side + 1) * CAP, :],
                                                            hT_e[:, j, hf * CAP:(hf + 1) * CAP], w[:, j, col:col + BANK],
                                                            start=(hf + j == 0), stop=(hf + j == 2), skip_group_check=True)
                        last.then_inc(s["y_full" if hf else "down0_used"], 1)

                all_drained(pe, f"xT{lay + 1}" if lay == 0 else f"pos{lay}")
                gather(0, 0)
                for i in range(2):
                    expert(0, i, True, False)
                n_pairs = n_r * PAIRS
                with pe.Fori(1, n_pairs - 1) as q:
                    for i in range(2):
                        expert(q, i, False, False)
                q = n_pairs - 1
                for i in range(2):
                    expert(q, i, False, True)
                pe.wait_ge(s["y_ready"], 2 * n_pairs)
                pe.wait_ge(s["xc_drained"], 6 * q + 6)
                for t8 in range(8):
                    scatter_tile(2 * q + 1, t8)
                pe.wait_ge(s["sc_drained"], 16 * n_pairs)

            experts(0)

            pe.wait_ge(h_ready, 2 * TT)
            transpose_hidden("xT1", h)
            wait_hT("xT1")
            drained_before(pe, "small1", 0)
            pe.wait_ge(small1_loaded, 16)
            for tt in range(TT):
                for k in range(KT):
                    last = nc.tensor.matmul(tile("small1")[:, tt * P:tt * P + 80], hT[:, k, tt * P:(tt + 1) * P], w_small1[:, k, :],
                                            start=(k == 0), stop=(k == KT - 1))
            last.then_inc(psum_full, 1)
            for c in range(8):
                chunk_natural(1, c)
            pe.wait_ge(roped, 1)
            for i in range(9):
                heads = [hd for hd in (2 * i, 2 * i + 1) if hd < IH + 1]
                transposes("qiT", i, [QIN[:, tt, hd, :] for hd in heads for tt in range(TT)])
            pe.wait_ge(roped, 2)
            for i in range(10):
                transposes("qkT", i, [QN[:, tt, hd, :] for hd in (2 * i, 2 * i + 1) for tt in range(TT)])
            wait_t = first["qkT"] + 9
            for who in "AD":
                pe.wait_ge(drained[who], drained_by[:wait_t + 1].count(who))
            for i in range(12):
                drained_before(pe, "index", i)
                tt, hs, nk = (1, range(2 * i, 2 * i + 2), SEQ) if i < 8 else (0, range(4 * (i - 8), 4 * (i - 8) + 4), P)
                for n, hd in enumerate(hs):
                    last = nc.tensor.matmul(tile("index", i)[:, n * nk:(n + 1) * nk], qiT[0:IDH, hd, tt * P:(tt + 1) * P],
                                            qiT[0:IDH, IH, 0:nk], start=True, stop=True)
                last.then_inc(psum_full, 1)

            groups = [(tt, g) for tt in range(TT) for g in range(KVH)]

            def attn_scores(n):
                tt, g = groups[n]
                nk = P * (tt + 1)
                per = BANK // nk
                for i in range(GQ // per):
                    drained_before(pe, f"S{tt}_{g}", i)
                    for j in range(per):
                        last = nc.tensor.matmul(tile(f"S{tt}_{g}", i)[:, j * nk:(j + 1) * nk],
                                                qT[:, GQ * g + per * i + j, tt * P:(tt + 1) * P], qT[:, AH + g, 0:nk],
                                                start=True, stop=True)
                    last.then_inc(psum_full, 1)

            attn_scores(0)
            for n, (tt, g) in enumerate(groups):
                if n + 1 < len(groups):
                    attn_scores(n + 1)
                pe.wait_ge(P_ready, n + 1)
                for kt in range(tt + 1):
                    transposes(f"PT{tt}_{g}", kt, [X[n % 2][:, j, kt * P:(kt + 1) * P] for j in range(GQ)])
                t = first[f"PT{tt}_{g}"] + tt
                pe.wait_ge(drained["A"], drained_by[:t + 1].count("A"))
                drained_before(pe, f"O{tt}_{g}", 0)
                for kt in range(tt + 1):
                    last = nc.tensor.matmul(tile(f"O{tt}_{g}")[:, :], VN[:, kt, g, :], PT[n % 2][:, kt, :],
                                            start=(kt == 0), stop=(kt == tt))
                last.then_inc(psum_full, 1)
            t = first["out1"] - 1
            pe.wait_ge(drained["A"], drained_by[:t + 1].count("A"))
            for c in range(8, 12):
                chunk_natural(1, c)
            experts(1)

        @block.scalar
        def _(act):
            step = [0]

            def link(ins):
                step[0] += 1
                ins.then_inc(act_s, 1)
                act.wait_ge(act_s, step[0])

            def hT_tiles(stage):
                for i in range(0, 8, 2):
                    act.wait_ge(psum_full, filled(stage, i))
                    act.activation(hT[:, 2 * i:2 * i + 2, :].rearrange("p a b -> p (a b)"), tile(stage, i)[:, :], ACT.Copy)\
                       .then_inc(drained["A"], 1)

            hT_tiles("xT0")
            act.wait_ge(psum_full, filled("gates", 1))
            act.activation(t3[0:RANK, 0:SEQ], tile("gates", 1)[0:RANK, 0:SEQ], ACT.Copy).then_inc(drained["A"], 1)
            act.wait_ge(lf_abs, 1)
            link(act.activation(row["ab"], row["xf"], ACT.Abs))
            link(act.activation(row["ab"], row["ab"], ACT.Exp, scale=-1.0))
            act.activation(row["ab"], row["ab"], ACT.Ln, bias=1.0).then_inc(lf_log, 1)
            act.wait_ge(rows_done, 1)
            act.activation(row["e"], row["m"], ACT.Exp, scale=-1.0).then_inc(e_done, 1)
            for j in range(8):
                act.wait_ge(conv_done, j + 1)
                act.activation(QKT[:, j, :], QKT[:, j, :], ACT.Silu).then_inc(qk_silu, 1)
            for c in (2, 3):
                for j in range(4):
                    act.wait_ge(psum_full, filled(f"chunk0_{c}", j))
                    act.activation(QKT[:, 4 * c + j, :], tile(f"chunk0_{c}", j)[:, 0:SEQ], ACT.Copy,
                                   scale=(DK ** -0.5 if c == 2 else 1.0)).then_inc(drained["A"], 1)
            act.wait_ge(gla_x, 1)
            link(act.activation(t2[:, :], t1[:, :], ACT.Abs))
            link(act.activation(t2[:, :], t2[:, :], ACT.Exp, scale=-1.0))
            act.activation(t2[:, :], t2[:, :], ACT.Ln, bias=1.0).then_inc(gla_log, 1)

            def values(c):
                for tt in range(TT):
                    act.wait_ge(psum_full, filled(f"chunk0_{c}", tt))
                    src = tile(f"chunk0_{c}", tt)[:, :]
                    if c in (4, 5, 8, 9):
                        hd = {4: 0, 5: 2, 8: 4, 9: 6}[c]
                        dst = V[:, tt, hd:hd + 2, 0:DV]
                        src = src.rearrange("p (a b) -> p a b", a=2)
                    else:
                        col = {6: 0, 7: 512, 10: 1024, 11: 1536}[c]
                        dst = mix[:, tt, col:col + 512]
                    ins = act.activation(dst, src, ACT.Copy)
                    ins.then_inc(drained["A"], 1)

            def mlstm_exp(hd):
                act.wait_ge(D_ready, hd + 1)
                act.wait_ge(cols_done, 1)
                w = Dl[:, hd % 2, :]
                act.activation(w[:, 0:SEQ], w[:, 0:SEQ], ACT.Exp, bias=gcol[:, 0, hd:hd + 1])
                act.activation(w[:, SEQ:SEQ + P], w[:, SEQ:SEQ + P], ACT.Exp, bias=gcol[:, 1, hd:hd + 1]).then_inc(E_ready, 1)

            def mlstm_square(hd):
                for tt in range(TT):
                    n = tt * NH + hd
                    act.wait_ge(hn_ready, TT * hd + tt + 1)
                    if hd + tt > 0:
                        act.wait_ge(ssq_ready, TT * hd + tt)
                    act.activation(t2[:, 0:DV], hn[:, n, :], ACT.Square, accum_out=ssq[:, n:n + 1]).then_inc(ssq_ready, 1)

            values(4)
            act.wait_ge(la_done, 1)
            act.activation(t1[:, :], la[:, :], ACT.Exp, scale=1.0 / 16).then_inc(gla_exp, 1)
            act.activation(t2[:, :], la[:, :], ACT.Exp, scale=-1.0 / 16).then_inc(gla_exp, 1)
            act.activation(decay[:, :], la_last[:, :], ACT.Exp)
            for n in range(NH * 4):
                sl = slice(n * CH, (n + 1) * CH)
                last = act.activation(t3[:, sl], la[:, sl], ACT.Exp, bias=la_last[:, n:n + 1], scale=-1.0 / 16)
            last.then_inc(gla_exp, 1)
            values(5)
            values(6)
            mlstm_exp(0)
            for hd in range(1, NH):
                values(6 + hd)
                if hd == 1:
                    act.wait_ge(qdec_done, 2)
                mlstm_square(hd - 1)
                mlstm_exp(hd)
            act.wait_ge(kz_zero, 1)
            for tt in range(TT):
                act.wait_ge(psum_full, filled("kend", tt))
                src = tile("kend", tt)[:, :].rearrange("p (h d) -> p h d", h=NH)
                act.activation(kz[0:CH, tt * NH:(tt + 1) * NH, 0, :], src[0:CH], ACT.Copy)
                act.activation(kz[CH:P, tt * NH:(tt + 1) * NH, 1, :], src[CH:P], ACT.Copy).then_inc(drained["A"], 1)
            values(10)
            mlstm_square(NH - 1)
            values(11)
            t = first["chunk0_11"] + 1
            act.wait_ge(drained["A"], drained_by[:t + 1].count("A"))
            act.activation(mix[:, :, 0:1024], mix[:, :, 0:1024], ACT.Sigmoid).then_inc(gates_done, 1)
            act.activation(mix[:, :, 1024:2048], mix[:, :, 1024:2048], ACT.Silu).then_inc(gates_done, 1)
            act.wait_ge(mlstm_mixed, 1)
            for i in range(4):
                tt, hp = i // 2, i % 2
                act.wait_ge(psum_full, filled("gO", i))
                for j in range(2):
                    n = tt * NH + 2 * hp + j
                    src = tile("gO", i)[:, j * DV:(j + 1) * DV]
                    act.activation(hn[:, n, :], src, ACT.Copy).then_inc(hn_ready, 1)
                    if j == 0:
                        act.wait_ge(ssq_ready, TT * NH + i)
                        if i:
                            act.wait_ge(drained["A"], drained_by[:first["gO"] + i].count("A"))
                    last = act.activation(t2[:, j * DV:(j + 1) * DV], src, ACT.Square, accum_out=ssq[:, TT * NH + n:TT * NH + n + 1])
                    if j == 0:
                        last.then_inc(ssq_ready, 1)
                    else:
                        last.then_inc(drained["A"], 1)
            hT_tiles("mixT0")

            def experts(lay):
                s = M[lay]
                hT_tiles(f"moeT{lay}")
                act.wait_ge(logits_ready, lay + 1)
                act.activation(aff[:, :, :], aff[:, :, :], ACT.Sigmoid).then_inc(aff_ready, 1)
                act.wait_ge(routed, lay + 1)
                n_r = act.value_load(rounds_i[0:1, 0:1], min_val=0, max_val=MAX_ROUNDS - 1) + 1

                def gathered(tiles_before):
                    for g in range(4):
                        act.wait_ge(s["xc_full"], tiles_before + g + 1)
                        act.activation(xcT[:, 4 * g:4 * g + 4, :].rearrange("p a b -> p (a b)"), ps[4 + g % 2][:, :], ACT.Copy)\
                           .then_inc(s["xc_drained"], 1)

                def expert(q, i, is_first, is_last):
                    x = 2 * q + i
                    begun = not (is_first and i == 0)
                    act.wait_ge(s["gate_full"], x + 1)
                    if begun:
                        act.wait_ge(s["h_ready"], x)
                    act.activation(silu_g[:, :], ps[0][:, 0:DV], ACT.Silu).then_inc(s["silu_ready"], 1)
                    act.wait_ge(s["hT_full"], x + 1)
                    if begun:
                        act.wait_ge(s["y_full"], x)
                    act.activation(hT_e[:, :, :].rearrange("p a b -> p (a b)"), ps[0][:, 0:2 * P], ACT.Copy)\
                       .then_inc(s["hT_ready"], 1)
                    act.wait_ge(s["xc_full"], 6 * q + 5 + i)
                    if begun:
                        act.wait_ge(s["sc_full"], 8 * x)
                    act.activation(pw_T[:, :, :, :].rearrange("p a b c -> p (a b c)"), ps[4 + i][:, :], ACT.Copy)\
                       .then_inc(s["xc_drained"], 1)
                    if i == 1 and not is_last:
                        gathered(6 * q + 6)
                    act.wait_ge(s["y_full"], x + 1)
                    act.activation(y_sb[:, 0:BANK], ps[2][:, :], ACT.Copy)
                    act.activation(y_sb[:, BANK:2 * BANK], ps[3][:, :], ACT.Copy).then_inc(s["y_ready"], 1)

                gathered(0)
                for i in range(2):
                    expert(0, i, True, False)
                with act.Fori(1, n_r * PAIRS - 1) as q:
                    for i in range(2):
                        expert(q, i, False, False)
                for i in range(2):
                    expert(n_r * PAIRS - 1, i, False, True)

            experts(0)

            hT_tiles("xT1")
            act.wait_ge(trig_in, 1)
            act.activation(sinv[:, :, :].rearrange("p a b -> p (a b)"), kf[:, 0, :], ACT.Sin)
            act.activation(cosv[:, :, :].rearrange("p a b -> p (a b)"), kf[:, 1, :], ACT.Sin).then_inc(trig_out, 1)
            for c in range(8):
                for tt in range(TT):
                    act.wait_ge(psum_full, filled(f"chunk1_{c}", tt))
                    src = tile(f"chunk1_{c}", tt)[:, :]
                    if c < 2:
                        dst = QIN[:, tt, 8 * c:8 * c + 8, :].rearrange("p a b -> p (a b)")
                    elif c == 2:
                        dst = QN[:, tt, AH:AH + KVH, :].rearrange("p a b -> p (a b)")
                    elif c == 3:
                        dst = VN[:, tt, :, :].rearrange("p a b -> p (a b)")
                    else:
                        dst = QN[:, tt, 4 * (c - 4):4 * (c - 3), :].rearrange("p a b -> p (a b)")
                    act.activation(dst, src, ACT.Copy).then_inc(drained["A"], 1)
            for i in range(0, 9, 2):
                act.wait_ge(psum_full, filled("qiT", i))
                n = 2 if i < 8 else 1
                act.activation(qiT[0:IDH, 2 * i:2 * i + n, :].rearrange("p a b -> p (a b)"), tile("qiT", i)[0:IDH, 0:n * SEQ],
                               ACT.Copy).then_inc(drained["A"], 1)
            for i in range(0, 10, 2):
                act.wait_ge(psum_full, filled("qkT", i))
                act.activation(qT[:, 2 * i:2 * i + 2, :].rearrange("p a b -> p (a b)"), tile("qkT", i)[:, :], ACT.Copy)\
                   .then_inc(drained["A"], 1)
            groups = [(tt, g) for tt in range(TT) for g in range(KVH)]

            def exps(n):
                tt, g = groups[n]
                nk = P * (tt + 1)
                act.wait_ge(X_ready, n + 1)
                for j in range(GQ):
                    last = act.activation(X[n % 2][:, j, 0:nk], X[n % 2][:, j, 0:nk], ACT.Exp, bias=mx[:, n % 2, GQ + j:GQ + j + 1],
                                          accum_out=mx[:, n % 2, 2 * GQ + j:2 * GQ + j + 1])
                last.then_inc(exp_ready, 1)

            exps(0)
            for n, (tt, g) in enumerate(groups):
                if n + 1 < len(groups):
                    exps(n + 1)
                for kt in range(tt + 1):
                    act.wait_ge(psum_full, filled(f"PT{tt}_{g}", kt))
                    act.activation(PT[n % 2][:, kt, :], tile(f"PT{tt}_{g}", kt)[:, :], ACT.Copy).then_inc(drained["A"], 1)
                act.wait_ge(psum_full, filled(f"O{tt}_{g}"))
                act.activation(hT[:, GQ * g:GQ * (g + 1), tt * P:(tt + 1) * P],
                               tile(f"O{tt}_{g}")[:, :].rearrange("p (a b) -> p a b", a=GQ), ACT.Copy).then_inc(drained["A"], 1)
            experts(1)

        @block.vector
        def _(v):
            step = [0]

            def link(ins):
                step[0] += 1
                ins.then_inc(dve, 1)
                v.wait_ge(dve, step[0])

            def hT_tiles(stage):
                for i in range(1, 8, 2):
                    v.wait_ge(psum_full, filled(stage, i))
                    v.tensor_copy(hT[:, 2 * i:2 * i + 2, :].rearrange("p a b -> p (a b)"), tile(stage, i)[:, :])\
                     .then_inc(drained["D"], 1)

            v.wait_ge(consts_ready, 1)
            hT_tiles("xT0")
            v.wait_ge(psum_full, filled("rows"))
            link(v.tensor_copy(small_cols[:, :], tile("rows")[:, 0:TAPS * 8 + 4]))
            v.engine_nop().then_inc(drained["D"], 1)
            v.wait_ge(psum_full, filled("gates", 0))
            v.wait_ge(small_loaded, 16 * 12)
            r = row
            v.memset(r["one"], 1.0)
            v.tensor_scalar(r["ig"], tile("gates")[0:NH, 0:SEQ], gate_bias[:, 0:1], None, ALU.add)
            link(v.tensor_scalar(r["xf"], tile("gates")[0:NH, SEQ:2 * SEQ], gate_bias[:, 1:2], None, ALU.add))
            v.engine_nop().then_inc(drained["D"], 1)
            v.engine_nop().then_inc(lf_abs, 1)
            v.wait_ge(lf_log, 1)
            link(v.scalar_tensor_tensor(r["lf"], r["xf"], 0.0, r["ab"], ALU.min, ALU.subtract))
            link(v.tensor_tensor_scan(r["b"], r["one"], r["lf"], 0.0, ALU.mult, ALU.add))
            link(v.tensor_tensor(r["g"], r["ig"], r["b"], ALU.subtract))
            link(v.tensor_tensor_scan(r["M"], r["g"], r["g"], 0.0, ALU.max, ALU.max))
            v.tensor_scalar(r["nM"], r["M"], -1.0, None, ALU.mult)
            v.tensor_tensor(r["m"], r["b"], r["M"], ALU.add).then_inc(rows_done, 1)
            for c in range(2):
                for j in range(4):
                    n = 4 * c + j
                    v.wait_ge(psum_full, filled(f"chunk0_{c}", j))
                    src = tile(f"chunk0_{c}", j)
                    tap = [small_cols[:, t * 8 + n:t * 8 + n + 1] for t in range(TAPS)]
                    link(v.tensor_scalar(QKT[:, n, :], src[:, 0:SEQ], tap[TAPS - 1], None, ALU.mult))
                    for back in range(1, TAPS):
                        dst = QKT[:, n, back:SEQ]
                        ins = v.scalar_tensor_tensor(dst, src[:, 0:SEQ - back], tap[TAPS - 1 - back], dst, ALU.mult, ALU.add)
                        if back < TAPS - 1:
                            link(ins)
                        else:
                            ins.then_inc(drained["D"], 1)
                    v.wait_ge(drained["D"], drained_by[:first[f"chunk0_{c}"] + j + 1].count("D"))
                    v.engine_nop().then_inc(conv_done, 1)
            for i in range(2):
                v.wait_ge(psum_full, filled("decay", i))
                for j in range(2):
                    hd = 2 * i + j
                    ins = v.tensor_scalar(t1[:, hd * SEQ:(hd + 1) * SEQ], tile("decay", i)[:, j * SEQ:(j + 1) * SEQ],
                                          small_cols[:, 32 + hd:33 + hd], None, ALU.add)
                ins.then_inc(drained["D"], 1)
            v.wait_ge(drained["D"], drained_by[:first["decay"] + 2].count("D"))
            v.engine_nop().then_inc(gla_x, 1)
            v.wait_ge(psum_full, filled("gcols"))
            v.tensor_copy(gcol[:, :, :], tile("gcols")[:, :].rearrange("p (a b) -> p a b", a=4)[:, :, 0:NH]).then_inc(drained["D"], 1)
            v.wait_ge(drained["D"], drained_by[:first["gcols"] + 1].count("D"))
            v.engine_nop().then_inc(cols_done, 1)
            v.wait_ge(gla_log, 1)
            link(v.scalar_tensor_tensor(t1[:, :], t1[:, :], 0.0, t2[:, :], ALU.min, ALU.subtract))
            link(v.tensor_tensor_scan(la[:, :], resets[:, :], t1[:, :], 0.0, ALU.mult, ALU.add))
            v.tensor_scalar(la_last[:, :], la[:, :].rearrange("p (n c) -> p n c", c=CH)[:, :, CH - 1], 1.0 / 16, None, ALU.mult)\
             .then_inc(la_done, 1)
            flat = QKT[:, :, :].rearrange("p a b -> p (a b)")
            gq, gk = flat[:, 8 * SEQ:12 * SEQ], flat[:, 12 * SEQ:16 * SEQ]
            t = first["chunk0_3"] + 3
            v.wait_ge(drained["A"], drained_by[:t + 1].count("A"))
            v.wait_ge(gla_exp, 1)
            v.tensor_tensor(gq, gq, t1[:, :], ALU.mult).then_inc(qdec_done, 1)
            v.wait_ge(gla_exp, 3)
            v.tensor_tensor(t3[:, :], t3[:, :], gk, ALU.mult).then_inc(kend_done, 1)
            v.tensor_tensor(gk, gk, t2[:, :], ALU.mult).then_inc(qdec_done, 1)

            def mlstm_weights(hd):
                v.wait_ge(psum_full, filled(f"mS{hd}", 0))
                if hd >= 2:
                    v.wait_ge(psum_full, filled(f"mO{hd - 2}", 1))
                mb = tile(f"mS{hd}", 0)
                d = Dl[:, hd % 2, :]
                v.tensor_tensor(d[:, 0:SEQ], mb[:, 0:SEQ], maskT[:, :], ALU.add)
                link(v.tensor_tensor(d[:, SEQ:SEQ + P], mb[:, P:2 * P], maskT[:, 0:P], ALU.add))
                v.engine_nop().then_inc(drained["D"], 1)
                v.engine_nop().then_inc(D_ready, 1)
                v.wait_ge(psum_full, filled(f"mS{hd}", 1))
                v.wait_ge(E_ready, hd + 1)
                link(v.scalar_tensor_tensor(W[:, hd % 2, :], tile(f"mS{hd}", 1)[:, 0:384], DK ** -0.5, d, ALU.mult, ALU.mult))
                v.engine_nop().then_inc(drained["D"], 1)
                v.engine_nop().then_inc(W_ready, 1)

            def mlstm_normalise(hd):
                for tt in range(TT):
                    v.wait_ge(psum_full, filled(f"mO{hd}", tt))
                    t = tile(f"mO{hd}", tt)
                    link(v.tensor_scalar(den_r[:, 2:3], t[:, DV:DV + 1], -1.0, None, ALU.mult))
                    link(v.scalar_tensor_tensor(den_r[:, 0:1], t[:, DV:DV + 1], gcol[:, 2 + tt, hd:hd + 1], den_r[:, 2:3], ALU.max, ALU.max))
                    link(v.reciprocal(den_r[:, 1:2], den_r[:, 0:1]))
                    link(v.tensor_scalar(hn[:, tt * NH + hd, :], t[:, 0:DV], den_r[:, 1:2], None, ALU.mult))
                    v.engine_nop().then_inc(drained["D"], 1)
                    v.engine_nop().then_inc(hn_ready, 1)

            def head_norm(br):
                sl = slice(br * TT * NH, (br + 1) * TT * NH)
                v.tensor_scalar(ssq_m[:, sl], ssq[:, sl], 1.0 / DV, HN_EPS, ALU.mult, ALU.add).then_inc(ssq_scaled, 1)
                v.wait_ge(hr_ready, br + 1)
                for n in range(TT * NH):
                    g = norm_g[:, br * 1024 + (n % NH) * DV:br * 1024 + (n % NH + 1) * DV]
                    ins = v.scalar_tensor_tensor(hn[:, n, :], hn[:, n, :], hn_r[:, br * 8 + n:br * 8 + n + 1], g, ALU.mult, ALU.mult)
                link(ins)
                v.wait_ge(gates_done, br + 1)
                m = mix[:, :, br * 1024:(br + 1) * 1024]
                v.tensor_tensor(m, m, hn[:, :, :].rearrange("p (t h) d -> p t (h d)", t=TT), ALU.mult)\
                 .then_inc(mlstm_mixed if br == 0 else mix_ready, 1)

            mlstm_weights(0)
            for hd in range(1, NH):
                mlstm_normalise(hd - 1)
                mlstm_weights(hd)
            mlstm_normalise(NH - 1)
            v.memset(kz[:, :, :, :].rearrange("p a b c -> p (a b c)"), 0.0).then_inc(kz_zero, 1)
            link(v.memset(attnT[:, :, :].rearrange("p a b -> p (a b)"), 0.0))
            for tt in range(TT):
                v.wait_ge(psum_full, filled("gattn", tt))
                link(v.copy_predicated(attnT[:, tt * NH:(tt + 1) * NH, :], chunk_mask.unsqueeze(1).broadcast_to([P, NH, P]),
                                       tile("gattn", tt)[:, :].rearrange("p (a b) -> p a b", a=NH)))
                v.engine_nop().then_inc(drained["D"], 1)
                v.engine_nop().then_inc(attn_ready, 1)
            for c in range(3):
                for hp in range(2):
                    i = 2 * c + hp
                    v.wait_ge(psum_full, filled("gstate", i))
                    for j in range(2):
                        hd = 2 * hp + j
                        src = tile("gstate", i)[:, j * DV:(j + 1) * DV]
                        if c == 0:
                            ins = v.tensor_copy(state[:, 0, hd, :], src)
                        else:
                            ins = v.scalar_tensor_tensor(state[:, c, hd, :], state[:, c - 1, hd, :],
                                                         decay[:, hd * 4 + c:hd * 4 + c + 1], src, ALU.mult, ALU.add)
                    link(ins)
                    v.engine_nop().then_inc(drained["D"], 1)
                    v.engine_nop().then_inc(state_ready, 1)
            v.wait_ge(ssq_ready, TT * NH)
            head_norm(0)
            v.wait_ge(ssq_ready, TT * NH + 4)
            t = first["gO"] + 3
            v.wait_ge(drained["A"], drained_by[:t + 1].count("A"))
            head_norm(1)
            hT_tiles("mixT0")

            def residual(lay):
                for i in range(8):
                    c, tt = i // 2, i % 2
                    v.wait_ge(psum_full, filled(f"out{lay}", i))
                    d = h[:, tt, c * BANK:(c + 1) * BANK]
                    v.scalar_tensor_tensor(d, d, ALPHA, tile(f"out{lay}", i)[:, :], ALU.mult, ALU.add).then_inc(drained["D"], 1)
                v.wait_ge(drained["D"], drained_by[:first[f"out{lay}"] + 8].count("D"))

            def layer_norm(n, src):
                for tt in range(TT):
                    for c in range(4):
                        ins = v.bn_stats(stats[:, tt, c, :], src[:, tt, c * BANK:(c + 1) * BANK])
                link(ins)
                for tt in range(TT):
                    ins = v.bn_aggr(mean_var[:, tt, :], stats[:, tt, :, :].rearrange("p a b -> p (a b)"))
                link(ins)
                v.tensor_scalar(var_eps[:, :], mean_var[:, :, 1], LN_EPS, None, ALU.add).then_inc(var_ready, 1)
                v.wait_ge(rstd_ready, n + 1)
                v.wait_ge(ln_loaded, 32 * (n + 1))
                for tt in range(TT):
                    ins = v.tensor_scalar(h[:, tt, :], src[:, tt, :], mean_var[:, tt, 0:1], rstd[:, tt:tt + 1], ALU.subtract, ALU.mult)
                link(ins)
                for tt in range(TT):
                    ins = v.tensor_tensor(h[:, tt, :], h[:, tt, :], ln_gb[:, 0, :], ALU.mult)
                link(ins)
                for tt in range(TT):
                    v.tensor_tensor(h[:, tt, :], h[:, tt, :], ln_gb[:, 1, :], ALU.add).then_inc(h_ready, 1)
                v.wait_ge(h_ready, TT * (n + 1))

            def ranks(dst, src, n_sets, a, b):
                s3 = src.rearrange("p t (g e) -> p (t g) e", e=4)
                d3 = dst.rearrange("p t (g e) -> p (t g) e", e=4)
                a3 = a.rearrange("p t (g e) -> p (t g) e", e=4)
                link(v.memset(dst, 0.0))
                for shift in range(1, 4):
                    n = 4 - shift
                    v.tensor_tensor(a3[:, :, 0:n], s3[:, :, shift:4], s3[:, :, 0:n], ALU.is_gt)
                    link(v.tensor_tensor(b.rearrange("p t (g e) -> p (t g) e", e=4)[:, :, 0:n], s3[:, :, 0:n], s3[:, :, shift:4], ALU.is_ge))
                    link(v.tensor_tensor(d3[:, :, 0:n], d3[:, :, 0:n], a3[:, :, 0:n], ALU.add))
                    link(v.tensor_tensor(d3[:, :, shift:4], d3[:, :, shift:4],
                                         b.rearrange("p t (g e) -> p (t g) e", e=4)[:, :, 0:n], ALU.add))

            def experts(lay):
                s = M[lay]
                hT_tiles(f"moeT{lay}")
                v.wait_ge(psum_full, filled(f"route{lay}"))
                link(v.tensor_copy(aff[:, :, :].rearrange("p a b -> p (a b)"), tile(f"route{lay}")[:, 0:TT * NE]))
                v.engine_nop().then_inc(drained["D"], 1)
                v.engine_nop().then_inc(logits_ready, 1)
                v.wait_ge(aff_ready, lay + 1)
                link(v.tensor_tensor(sel[:, :, :], aff[:, :, :], router_b[:, :].unsqueeze(1).broadcast_to([P, TT, NE]), ALU.add))
                s3 = sel[:, :, :].rearrange("p t (g e) -> p (t g) e", e=EPG)
                v.tensor_tensor(pairs6[:, :, 0:3], s3[:, :, 0:3], s3[:, :, 1:4], ALU.add)
                v.tensor_tensor(pairs6[:, :, 3:5], s3[:, :, 0:2], s3[:, :, 2:4], ALU.add)
                link(v.tensor_tensor(pairs6[:, :, 5:6], s3[:, :, 0:1], s3[:, :, 3:4], ALU.add))
                link(v.reduce_max(gsc[:, :, :].rearrange("p a b -> p (a b)"), pairs6[:, :, :], AX.X))
                ranks(rank[:, :, :], sel[:, :, :], TT * NG, cmp[:, :, :], cmp2[:, :, :])
                ranks(grank[:, :, :], gsc[:, :, :], TT, cmp[:, :, 0:NG], cmp2[:, :, 0:NG])
                link(v.tensor_scalar(cmp[:, :, 0:NG], grank[:, :, :], 0.5, None, ALU.is_lt))
                link(v.tensor_scalar(cmp2[:, :, :], rank[:, :, :], 1.5, None, ALU.is_lt))
                for tt in range(TT):
                    ins = v.tensor_tensor(chosen[:, tt, :].rearrange("p (g e) -> p g e", e=EPG),
                                          cmp2[:, tt, :].rearrange("p (g e) -> p g e", e=EPG),
                                          cmp[:, tt, 0:NG].unsqueeze(2).broadcast_to([P, NG, EPG]), ALU.mult)
                link(ins)
                v.engine_nop().then_inc(mask_ready, 1)
                link(v.tensor_tensor(sel[:, :, :], aff[:, :, :], chosen[:, :, :], ALU.mult))
                link(v.reduce_sum(csum[:, :, 0], sel[:, :, :], AX.X))
                link(v.reciprocal(crec[:, :, 0], csum[:, :, 0]))
                for tt in range(TT):
                    ins = v.tensor_scalar(sel[:, tt, :], sel[:, tt, :], crec[:, tt, :], None, ALU.mult)
                link(ins)
                v.wait_ge(psum_full, filled(f"pos{lay}"))
                t = tile(f"pos{lay}")
                link(v.scalar_tensor_tensor(rank[:, :, :], t[:, 0:2 * NE].rearrange("p (t e) -> p t e", t=TT), 1.0, chosen[:, :, :], ALU.add, ALU.mult))
                link(v.reduce_max(rounds_f[:, 0:1], t[:, 2 * NE:3 * NE], AX.X))
                v.engine_nop().then_inc(drained["D"], 1)
                for r_ in range(MAX_ROUNDS):
                    v.tensor_scalar(pos_r[:, :, r_ * NE:(r_ + 1) * NE], rank[:, :, :], -1.0 - CAP * r_, None, ALU.add)
                    v.tensor_copy(comb_r[:, :, r_ * NE:(r_ + 1) * NE], sel[:, :, :])
                link(v.tensor_scalar(rounds_f[:, 1:2], rounds_f[:, 0:1], CAP + 0.5, None, ALU.is_gt))
                for r_ in range(2, MAX_ROUNDS):
                    link(v.tensor_scalar(rounds_f[:, 2:3], rounds_f[:, 0:1], CAP * r_ + 0.5, None, ALU.is_gt))
                    link(v.tensor_tensor(rounds_f[:, 1:2], rounds_f[:, 1:2], rounds_f[:, 2:3], ALU.add))
                v.memset(pick_w[:, :, :, :].rearrange("p a b c -> p (a b c)"), 0.0)
                v.tensor_scalar(acc[:, :, :].rearrange("p a b -> p (a b)"), h[:, :, :].rearrange("p a b -> p (a b)"), ALPHA, None, ALU.mult)
                v.tensor_copy(rounds_i[:, :], rounds_f[:, 1:2]).then_inc(routed, 1)
                v.wait_ge(routed, lay + 1)
                n_r = v.value_load(rounds_i[0:1, 0:1], min_val=0, max_val=MAX_ROUNDS - 1) + 1

                def pick_tokens(pair):
                    for tt in range(TT):
                        for e in range(2):
                            ins = v.tensor_scalar(pick_p[:, tt, e * CAP:(e + 1) * CAP], slots64[:, :],
                                                  pos_r[:, tt, bass.ds(2 * pair + e, 1)], None, ALU.is_equal)
                    ins.then_inc(s["pick_ready"], 1)

                def add_tile(x, t8):
                    c, tt = t8 // 2, t8 % 2
                    v.wait_ge(s["sc_full"], 8 * x + t8 + 1)
                    d = acc[:, tt, c * BANK:(c + 1) * BANK]
                    v.tensor_tensor(d, ps[6 + t8 % 2][:, :], d, ALU.add).then_inc(s["sc_drained"], 1)

                def expert(q, i, is_first, is_last):
                    x = 2 * q + i
                    begun = not (is_first and i == 0)
                    if not is_first:
                        v.wait_ge(s["xc_full"], 6 * q + i - 1)
                    for tt in range(TT):
                        ins = v.tensor_scalar(pick_w[:, i, tt, CAP:2 * CAP], slots64[:, :], pos_r[:, tt, bass.ds(x, 1)],
                                              comb_r[:, tt, bass.ds(x, 1)], ALU.is_equal, ALU.mult)
                    ins.then_inc(s["pw_ready"], 1)
                    if i == 0 and not is_last:
                        v.wait_ge(s["xc_full"], 6 * q + 4)
                        pick_tokens(q + 1)
                    v.wait_ge(s["up_full"], x + 1)
                    v.wait_ge(s["silu_ready"], x + 1)
                    if begun:
                        v.wait_ge(s["hT_full"], x)
                    v.tensor_tensor(h_e[:, :], ps[1][:, 0:DV], silu_g[:, :], ALU.mult).then_inc(s["h_ready"], 1)
                    if begun:
                        for t8 in range(8):
                            add_tile(x - 1, t8)

                pick_tokens(0)
                for i in range(2):
                    expert(0, i, True, False)
                with v.Fori(1, n_r * PAIRS - 1) as q:
                    for i in range(2):
                        expert(q, i, False, False)
                q = n_r * PAIRS - 1
                for i in range(2):
                    expert(q, i, False, True)
                for t8 in range(8):
                    add_tile(2 * q + 1, t8)
                v.wait_ge(s["sc_drained"], 16 * (q + 1))

            residual(0)
            layer_norm(0, h)
            experts(0)
            layer_norm(1, acc)

            for half, at in ((16, 0), (8, 16)):
                f = np.float32(1) / (np.float32(500000.0) ** (np.arange(half, dtype=np.float32) / np.float32(half)))
                for n in range(half):
                    ins = v.memset(freq[:, at + n:at + n + 1], float(f[n]))
            link(v.tensor_copy(pos_f[:, :], pos_int[:, :]))
            for tt in range(TT):
                ins = v.tensor_scalar(angles[:, tt, :], freq[:, :], pos_f[:, tt:tt + 1], None, ALU.mult)
            link(ins)
            ang = angles[:, :, :].rearrange("p a b -> p (a b)")
            two_pi = 2 * math.pi
            c1 = 6.28125
            c2 = float(np.float32(round((two_pi - c1) * 2 ** 21) / 2 ** 21))
            c3 = float(np.float32(two_pi - c1 - c2))
            magic = 1.5 * 2 ** 23
            turn = [score[:, 0, 0:48], score[:, 0, 48:96]]
            for n, quarter in enumerate((0.0, 0.25)):
                v.tensor_scalar(turn[n], ang, float(np.float32(1 / two_pi)), quarter, ALU.mult, ALU.add)
            link(v.engine_nop())
            for n in range(2):
                ins = v.tensor_scalar(turn[n], turn[n], magic, None, ALU.add)
            link(ins)
            for n in range(2):
                ins = v.tensor_scalar(turn[n], turn[n], magic, None, ALU.subtract)
            link(ins)
            for m, cc in enumerate((c1, c2, c3)):
                for n in range(2):
                    ins = v.scalar_tensor_tensor(kf[:, n, :], turn[n], -cc, ang if m == 0 else kf[:, n, :], ALU.mult, ALU.add)
                link(ins)
            link(v.tensor_scalar(kf[:, 1, :], kf[:, 1, :], math.pi / 2, None, ALU.add))
            v.tensor_scalar(kf[:, :, :].rearrange("p a b -> p (a b)"), kf[:, :, :].rearrange("p a b -> p (a b)"), 3.1415925, -3.1415925, ALU.min, ALU.max)\
             .then_inc(trig_in, 1)
            hT_tiles("xT1")
            v.wait_ge(psum_full, filled("small1"))
            for tt in range(TT):
                v.tensor_copy(QIN[:, tt, IH, :], tile("small1")[:, tt * P:tt * P + IDH])
                ins = v.tensor_scalar(wi[:, tt, :], tile("small1")[:, tt * P + IDH:tt * P + 80], float(IH ** -0.5 * IDH ** -0.5), None, ALU.mult)
            ins.then_inc(drained["D"], 1)
            v.wait_ge(trig_out, 1)

            def rope(x, heads, half, at):
                x1, x2 = x[:, :, 0:heads, 0:half], x[:, :, 0:heads, half:2 * half]
                for tt in range(TT):
                    c = cosv[:, tt, at:at + half].unsqueeze(1).broadcast_to([P, heads, half])
                    s_ = sinv[:, tt, at:at + half].unsqueeze(1).broadcast_to([P, heads, half])
                    tmp = [rope_t[:, n, tt * heads * half:(tt + 1) * heads * half].rearrange("p (a b) -> p a b", b=half) for n in range(4)]
                    v.tensor_tensor(tmp[0], x1[:, tt], c, ALU.mult)
                    v.tensor_tensor(tmp[1], x2[:, tt], s_, ALU.mult)
                    v.tensor_tensor(tmp[2], x2[:, tt], c, ALU.mult)
                    ins = v.tensor_tensor(tmp[3], x1[:, tt], s_, ALU.mult)
                link(ins)
                for tt in range(TT):
                    tmp = [rope_t[:, n, tt * heads * half:(tt + 1) * heads * half].rearrange("p (a b) -> p a b", b=half) for n in range(4)]
                    v.tensor_tensor(x1[:, tt], tmp[0], tmp[1], ALU.subtract)
                    ins = v.tensor_tensor(x2[:, tt], tmp[2], tmp[3], ALU.add)
                ins.then_inc(roped, 1)

            t = first["chunk1_1"] + 1
            v.wait_ge(drained["A"], drained_by[:t + 1].count("A"))
            v.wait_ge(drained["D"], drained_by[:first["small1"] + 1].count("D"))
            v.wait_ge(psum_full, filled("small1"))
            rope(QIN, IH + 1, IDH // 8, 16)
            t = first["chunk1_7"] + 1
            v.wait_ge(drained["A"], drained_by[:t + 1].count("A"))
            v.wait_ge(roped, 1)
            rope(QN, AH + KVH, DH // 8, 0)
            for i in range(1, 9, 2):
                v.wait_ge(psum_full, filled("qiT", i))
                v.tensor_copy(qiT[0:IDH, 2 * i:2 * i + 2, :].rearrange("p a b -> p (a b)"), tile("qiT", i)[0:IDH, :])\
                 .then_inc(drained["D"], 1)
            for i in range(1, 10, 2):
                v.wait_ge(psum_full, filled("qkT", i))
                v.tensor_copy(qT[:, 2 * i:2 * i + 2, :].rearrange("p a b -> p (a b)"), tile("qkT", i)[:, :])\
                 .then_inc(drained["D"], 1)
            for tt, lo, hi in ((1, 0, 8), (0, 8, 12)):
                nk = P * (tt + 1)
                per = BANK // nk
                for i in range(lo, hi):
                    v.wait_ge(psum_full, filled("index", i))
                    h0 = per * (i - lo)
                    v.scalar_tensor_tensor(R[:, h0:h0 + per, 0:nk], tile("index", i)[:, :].rearrange("p (a b) -> p a b", a=per), 0.0,
                                           wi[:, tt, h0:h0 + per].unsqueeze(2).broadcast_to([P, per, nk]), ALU.max, ALU.mult)\
                     .then_inc(drained["D"], 1)
                v.wait_ge(drained["D"], drained_by[:first["index"] + hi].count("D"))
                link(v.reduce_sum(score[:, tt, 0:nk], R[:, :, 0:nk].rearrange("p a b -> p b a"), AX.X))
                link(v.tensor_tensor(work[:, tt, 0:nk], score[:, tt, 0:nk], maskN[:, SEQ - nk:SEQ], ALU.add))
            for _ in range(TOPK // 8):
                for tt in range(TT):
                    ins = v.max(top8[:, tt, :], work[:, tt, 0:P * (tt + 1)])
                link(ins)
                for tt in range(TT):
                    w_ = work[:, tt, 0:P * (tt + 1)]
                    ins = v.match_replace(w_, top8[:, tt, :], w_, TAKEN)
                link(ins)
            for tt in range(TT):
                w_ = work[:, tt, 0:P * (tt + 1)]
                ins = v.tensor_scalar(w_, w_, TAKEN / 2, NEG, ALU.is_gt, ALU.mult)
            link(ins)
            for tt in range(TT):
                w_ = work[:, tt, 0:P * (tt + 1)]
                ins = v.tensor_tensor(w_, w_, maskN[:, SEQ - P * (tt + 1):SEQ], ALU.add)
            link(ins)
            groups = [(tt, g) for tt in range(TT) for g in range(KVH)]

            def logits(n):
                tt, g = groups[n]
                nk = P * (tt + 1)
                per = BANK // nk
                if n >= 2:
                    pt, pg = groups[n - 2]
                    v.wait_ge(psum_full, filled(f"PT{pt}_{pg}", pt))
                for i in range(GQ // per):
                    v.wait_ge(psum_full, filled(f"S{tt}_{g}", i))
                    v.scalar_tensor_tensor(X[n % 2][:, per * i:per * (i + 1), 0:nk],
                                           tile(f"S{tt}_{g}", i)[:, :].rearrange("p (a b) -> p a b", a=per), DH ** -0.5,
                                           work[:, tt, 0:nk].unsqueeze(1).broadcast_to([P, per, nk]), ALU.mult, ALU.add)\
                     .then_inc(drained["D"], 1)
                v.wait_ge(drained["D"], drained_by[:first[f"S{tt}_{g}"] + GQ // per].count("D"))
                link(v.reduce_max(mx[:, n % 2, 0:GQ], X[n % 2][:, :, 0:nk], AX.X))
                v.tensor_scalar(mx[:, n % 2, GQ:2 * GQ], mx[:, n % 2, 0:GQ], -1.0, None, ALU.mult).then_inc(X_ready, 1)

            logits(0)
            for n, (tt, g) in enumerate(groups):
                if n + 1 < len(groups):
                    logits(n + 1)
                nk = P * (tt + 1)
                v.wait_ge(exp_ready, n + 1)
                link(v.reciprocal(mx[:, n % 2, 0:GQ], mx[:, n % 2, 2 * GQ:3 * GQ]))
                for j in range(GQ):
                    ins = v.tensor_scalar(X[n % 2][:, j, 0:nk], X[n % 2][:, j, 0:nk], mx[:, n % 2, j:j + 1], None, ALU.mult)
                ins.then_inc(P_ready, 1)
            v.wait_ge(psum_full, filled("O1_3"))
            t = first["out1"] - 1
            v.wait_ge(drained["A"], drained_by[:t + 1].count("A"))
            v.engine_nop().then_inc(mixer1_done, 1)
            residual(1)
            layer_norm(2, h)
            experts(1)
            layer_norm(3, acc)


_INS = ["x", "positions", "ab_w_in", "ab_conv_w", "ab_igate_b", "ab_fgate_b", "ab_gla_gate_w2", "ab_gla_gate_b",
        "ab_mlstm_norm_g", "ab_gla_norm_g", "ab_w_out", "c_w_in", "c_w_out", "router_w", "router_bias",
        "moe_w_gate", "moe_w_up", "moe_w_down", "ln_mix_g", "ln_mix_b", "ln_ffn_g", "ln_ffn_b"]


def kernel(**inputs):
    import numpy as _np
    import concourse.bacc as _bacc
    from concourse import mybir as _mybir
    from concourse.bass_utils import run_bass_kernel_spmd as _run

    nc = _bacc.Bacc("TRN2", target_bir_lowering=False, num_devices=1)
    arrays, aps = {}, {}
    for name in _INS:
        x = _np.ascontiguousarray(inputs[name])
        arrays[f"in_{name}"] = x
        aps[name] = nc.dram_tensor(f"in_{name}", x.shape, _mybir.dt.from_np(x.dtype), kind="ExternalInput").ap()
    out = nc.dram_tensor("out", (1, SEQ, D), _mybir.dt.float32, kind="ExternalOutput").ap()
    program(nc, aps, out)
    r = _run(nc, [arrays], core_ids=[0])
    return r.results[0]["out"]
```

```python
import math
from contextlib import ExitStack

import numpy as np
import concourse.bass as bass
from concourse import mybir

FP32 = mybir.dt.float32
FP32R = mybir.dt.float32r
INT32 = mybir.dt.int32
ALU = mybir.AluOpType
ACT = mybir.ActivationFunctionType
AX = mybir.AxisListType

P = 128
SEQ, D = 256, 2048
TT = SEQ // P
KT = D // P
BANK = 512
SLOT = 4096
NH, DK, DV = 4, 128, 256
CH = 64
RANK = 16
TAPS = 4
AH, KVH, DH = 16, 4, 128
GQ = AH // KVH
IH, IDH = 16, 64
TOPK = min(256, SEQ // 4)
NE, NG, EPG, FF = 16, 4, 4, 512
CAP = 64
MAX_ROUNDS = SEQ // CAP
PAIRS = NE // 2
ALPHA = float((2 * 2) ** 0.25)
LN_EPS, HN_EPS = 1e-5, 1e-6
NEG = -1e30
TAKEN = -3e38

MQ, MK, MV, MI, MO, GQC, GK, GV, GLR, GR = 0, 512, 1024, 2048, 2056, 3080, 3592, 4104, 5128, 5144
AK, AV, QI, KI = 2048, 2560, 3072, 4096

L0_CHUNKS = [MQ, MK, GQC, GK, MV, MV + 512, MO, MO + 512, GV, GV + 512, GR, GR + 512]
L1_CHUNKS = [QI, QI + 512, AK, 0, 512, 1024, AV, 1536]
Q_CHUNK = [3, 4, 5, 7]
V_CHUNK = 6
OUT_CHUNKS = [0, 512, 1024, 1536]


def tile_plan():
    plan = [("xT0", 8, "ADADADAD"), ("rows", 1, "D"), ("gates", 1, "D")]
    plan += [(f"chunk0_{c}", 4, "DDDD" if c < 2 else "AAAA") for c in range(4)]
    plan += [("decay", 2, "DD"), ("gcols", 1, "D")]
    plan += [("chunk0_4", 2, "AA"), ("chunk0_5", 2, "AA"), ("chunk0_6", 2, "AA"), ("mS0", 2, "DD")]
    plan += [("chunk0_7", 2, "AA"), ("mO0", 2, "DD"), ("mS1", 2, "DD")]
    plan += [("chunk0_8", 2, "AA"), ("mO1", 2, "DD"), ("mS2", 2, "DD")]
    plan += [("chunk0_9", 2, "AA"), ("mO2", 2, "DD"), ("mS3", 2, "DD"), ("kend", 2, "AA"), ("mO3", 2, "DD")]
    plan += [("chunk0_10", 2, "AA"), ("gstate", 6, "DDDDDD"), ("gattn", 2, "DD"), ("gO", 4, "AAAA")]
    plan += [("chunk0_11", 2, "AA"), ("mixT0", 8, "D" * 8), ("out0", 8, "D" * 8)]
    plan += [("moeT0", 8, "ADADADAD"), ("route0", 2, "DD"), ("pos0", 1, "D")]
    plan += [("xT1", 8, "ADADADAD"), ("small1", 1, "D")]
    plan += [("chunk1_0", 2, "AA"), ("small1T", 1, "D"), ("chunk1_1", 2, "AA"), ("chunk1_2", 2, "AA")]
    plan += [("qiT", 9, "ADADADADA"), ("index", 12, "D" * 12), ("kT", 2, "AD")]
    plan += [("chunk1_3", 2, "AA"), ("chunk1_4", 2, "AA")]

    def heads_in(g):
        return [(f"qT{g}", 2, "AD"), (f"S0_{g}", 1, "D"), (f"S1_{g}", 2, "DD")]

    def heads_out(g):
        return [(f"PT0_{g}", 1, "A"), (f"O0_{g}", 1, "A"), (f"PT1_{g}", 2, "AA"), (f"O1_{g}", 1, "A")]

    plan += heads_in(0) + [("chunk1_5", 2, "AA")] + heads_in(1) + [("chunk1_6", 2, "AA")] + heads_out(0)
    plan += heads_in(2) + [("chunk1_7", 2, "AA")] + heads_out(1) + heads_in(3) + heads_out(2) + heads_out(3)
    plan += [("out1", 8, "D" * 8), ("moeT1", 8, "ADADADAD"), ("route1", 2, "DD"), ("pos1", 1, "D")]
    return plan


def program(nc, a, out):
    first, drained_by, n = {}, "", 0
    for stage, count, engines in tile_plan():
        assert len(engines) == count, stage
        first[stage] = n
        drained_by += engines
        n += count

    ctx = ExitStack()
    with ctx:
        def sbuf(name, shape, dt=FP32):
            return ctx.enter_context(nc.sbuf_tensor(name, shape, dt))

        def sem(name):
            return ctx.enter_context(nc.semaphore(name))

        def renamed(name, words, parts):
            with nc.sbuf_tensor(name, [P, words], FP32) as whole:
                pass
            over, at = [], 0
            for part, start, size in parts:
                if start > at:
                    sbuf(f"under_{part}", [P, start - at])
                over.append(sbuf(part, [P, size], FP32R))
                at = start + size
            if words > at:
                sbuf(f"rest_of_{name}", [P, words - at])
            return whole, over

        h = sbuf("h", [P, TT, D])
        hT, (x_hi,) = renamed("hT", KT * SEQ, [("x_hi", 0, KT * SEQ)])
        ring, (w_lo,) = renamed("ring", 3 * SLOT, [("w_lo", 0, 3 * SLOT)])
        W_HI, X_LO = TT * (2 * NH * (DV + 1) + D), 13184
        arena, (w_hi, x_lo) = renamed("arena", 18432, [("w_hi", W_HI, SLOT), ("x_lo", X_LO, KT * SEQ)])
        arena2 = sbuf("arena2", [P, 3 * SLOT])
        ident = sbuf("ident", [P, P])
        maskT = sbuf("maskT", [P, SEQ])
        maskN = sbuf("maskN", [P, SEQ])
        before = sbuf("before", [P, P])
        ones = sbuf("ones", [P, P])
        slots64 = sbuf("slots64", [P, CAP])
        router_w = sbuf("router_w", [P, KT, NE])
        router_b = sbuf("router_b", [P, NE])
        mhalf = sbuf("mhalf", [P, 16])
        stats = sbuf("stats", [P, TT, 4, 6])
        mean_var = sbuf("mean_var", [P, TT, 2])
        var_eps = sbuf("var_eps", [P, TT])
        rstd = sbuf("rstd", [P, TT])
        rounds_f = sbuf("rounds_f", [P, 4])
        rounds_i = sbuf("rounds_i", [P, 1], INT32)
        pos_int = sbuf("pos_int", [P, TT], INT32)
        small_rows = sbuf("small_rows", [TAPS * 8 + 4, P])
        small_cols = sbuf("small_cols", [P, TAPS * 8 + 4])
        gate_bias = sbuf("gate_bias", [32 + NH, 1])

        def slot(s):
            return ring[:, s * SLOT:(s + 1) * SLOT] if s < 3 else arena2[:, (s - 3) * SLOT:(s - 2) * SLOT]

        def carve(tensor, start, shape):
            size = 1
            for x in shape:
                size *= x
            assert start + size <= tensor.shape[1], (start, shape)
            v = tensor[:, start:start + size]
            if len(shape) == 2:
                v = v.rearrange("p (a b) -> p a b", b=shape[1])
            if len(shape) == 3:
                v = v.rearrange("p (a b c) -> p a b c", b=shape[1], c=shape[2])
            return v, start + size

        V, o = carve(arena, 0, [TT, 2 * NH, DV + 1])
        mix, o = carve(arena, o, [TT, D])
        QKT, o = carve(arena, o, [16, SEQ])
        norm_g, o = carve(arena, o, [D])
        w_small0, o = carve(arena, o, [KT, 24])
        w2, o = carve(arena, o, [NH * DK])
        pick, o = carve(arena, o, [NH, P])
        hn, o = carve(arena, o, [TT * NH, DV])
        ssq, o = carve(arena, o, [2 * TT * NH])
        hn_r, o = carve(arena, o, [2 * TT * NH])
        ssq_m, o = carve(arena, o, [2 * TT * NH])
        gcol, o = carve(arena, o, [4, NH])
        la_last, o = carve(arena, o, [NH * 4])
        decay, o = carve(arena, o, [NH * 4])
        den_r, o = carve(arena, o, [4])
        la, o = carve(arena2, 0, [NH * SEQ])
        t1, o = carve(arena2, o, [NH * SEQ])
        t2, o = carve(arena2, o, [NH * SEQ])
        t3, o = carve(arena2, o, [NH * SEQ])
        resets, o = carve(arena2, o, [NH * SEQ])
        kz_at = o
        kz, o = carve(arena2, o, [TT * NH, 2, DK])
        attnT, o = carve(arena2, o, [TT * NH, P])
        s_at = o
        state, o = carve(arena2, o, [3, NH, DV])
        Dl, k = carve(arena2, kz_at, [2, 384])
        W, k = carve(arena2, k, [2, 384])
        row = {}
        k = s_at
        for name in ("xf", "ab", "lf", "b", "ig", "g", "M", "nM", "m", "e", "one"):
            row[name], k = carve(arena2, k, [SEQ])
            row[name] = row[name][0:NH, :]
        chunk_mask = carve(arena2, o, [P])[0].bitcast(INT32)
        cmf, _ = carve(arena2, o + P, [P])

        hT = hT[:, :].rearrange("p (a b) -> p a b", b=SEQ)
        x_hi = x_hi[:, :].rearrange("p (a b) -> p a b", b=SEQ)
        x_lo = x_lo[:, :].rearrange("p (a b) -> p a b", b=SEQ)
        w_hi = w_hi[:, :].rearrange("p (a b) -> p a b", a=2)

        ln_gb, o = carve(arena, 0, [2, D])
        acc, o = carve(arena, o, [TT, D])
        xc_at = o
        xcT, o = carve(arena, o, [KT, 2 * CAP])
        y_sb, o = carve(arena, o, [2 * BANK])
        pick_p, o = carve(arena, o, [TT, 2 * CAP])
        pick_w, o = carve(arena, o, [2, TT, 3 * CAP])
        pw_T, o = carve(arena, o, [2, TT, P])
        silu_g, o = carve(arena, o, [DV])
        h_e, o = carve(arena, o, [DV])
        hT_e, o = carve(arena, o, [2, P])
        pos_r, o = carve(arena, o, [TT, MAX_ROUNDS * NE])
        comb_r, o = carve(arena, o, [TT, MAX_ROUNDS * NE])
        aff, k = carve(arena, xc_at, [TT, NE])
        sel, k = carve(arena, k, [TT, NE])
        rank, k = carve(arena, k, [TT, NE])
        cmp, k = carve(arena, k, [TT, NE])
        cmp2, k = carve(arena, k, [TT, NE])
        pairs6, k = carve(arena, k, [TT * NG, 6])
        gsc, k = carve(arena, k, [TT, NG])
        grank, k = carve(arena, k, [TT, NG])
        gcmp, k = carve(arena, k, [TT, NG])
        gcmp2, k = carve(arena, k, [TT, NG])
        chosen, k = carve(arena, k, [TT, NE])
        csum, k = carve(arena, k, [TT, 1])
        crec, k = carve(arena, k, [TT, 1])
        logits_T, k = carve(arena, k, [SEQ])

        QN, o = carve(arena, 0, [TT, (AH + KVH), DH])
        VN, o = carve(arena, o, [TT, KVH, DH])
        qT, o = carve(arena, o, [AH + KVH, SEQ])
        score, o = carve(arena, o, [TT, SEQ])
        work, o = carve(arena, o, [TT, SEQ])
        wi, o = carve(arena, o, [TT, IH])
        angles, o = carve(arena, o, [TT, 24])
        freq, o = carve(arena, o, [24])
        cosv, o = carve(arena, o, [TT, 24])
        sinv, o = carve(arena, o, [TT, 24])
        kf, o = carve(arena, o, [2, TT * 24])
        pos_f, o = carve(arena, o, [TT])
        top8, o = carve(arena, o, [TT, 8])
        mx, o = carve(arena, o, [TT, 3 * GQ])
        small_T = work[0:IDH + IH, 0, :]
        QIN, _ = carve(arena, o, [TT, IH + 1, IDH])
        assert o <= X_LO, o
        attn_T, o = carve(arena, X_LO, [AH, SEQ])
        qiT, o = carve(arena2, 0, [IH + 1, SEQ])
        w_small1, k = carve(arena2, o, [KT, 80])
        R, o2 = carve(arena2, o, [IH, SEQ])
        rope_t, k = carve(arena2, o, [4, TT * (IH + 1) * IDH // 8])
        X, k = [[None, None], [None, None]], o
        for parity in range(2):
            for tt in range(TT):
                X[parity][tt], k = carve(arena2, k, [GQ, P * (tt + 1)])
        PT = [None, None]
        for tt in range(TT):
            PT[tt], k = carve(arena2, k, [tt + 1, GQ * P])
        rope_q, k = carve(arena2, k, [4, TT * GQ * 16])

        ps = [ctx.enter_context(nc.psum_tensor(f"ps{i}", [P, BANK], FP32)) for i in range(8)]

        small_loaded = sem("small_loaded")
        x_loaded = sem("x_loaded")
        ln_loaded = sem("ln_loaded")
        small1_loaded = sem("small1_loaded")
        out_stored = sem("out_stored")
        consts_ready = sem("consts_ready")
        pool_step = sem("pool_step")
        psum_full = sem("psum_full")
        drained = {"A": sem("drained_by_act"), "D": sem("drained_by_dve")}
        half_used = [sem("half_used_0"), sem("half_used_1")]
        unit_loaded = [[sem(f"unit_loaded_{lay}_{s}") for s in range(3)] for lay in range(2)]
        dve = sem("dve_step")
        act_s = sem("act_step")
        h_ready = sem("h_ready")
        var_ready = sem("var_ready")
        rstd_ready = sem("rstd_ready")
        conv_done = sem("conv_done")
        qk_silu = sem("qk_silu")
        lf_abs = sem("lf_abs")
        lf_log = sem("lf_log")
        rows_done = sem("rows_done")
        e_done = sem("e_done")
        cols_done = sem("cols_done")
        gla_x = sem("gla_x")
        gla_log = sem("gla_log")
        la_done = sem("la_done")
        gla_exp = sem("gla_exp")
        qdec_done = sem("qdec_done")
        kend_done = sem("kend_done")
        kz_zero = sem("kz_zero")
        D_ready = sem("D_ready")
        E_ready = sem("E_ready")
        W_ready = sem("W_ready")
        hn_ready = sem("hn_ready")
        ssq_ready = sem("ssq_ready")
        ssq_scaled = sem("ssq_scaled")
        hr_ready = sem("hr_ready")
        gates_done = sem("gates_done")
        attn_ready = sem("attn_ready")
        state_ready = sem("state_ready")
        mlstm_mixed = sem("mlstm_mixed")
        mix_ready = sem("mix_ready")
        aff_ready = sem("aff_ready")
        logits_ready = sem("logits_ready")
        mask_ready = sem("mask_ready")
        routed = sem("routed")
        trig_in = sem("trig_in")
        trig_out = sem("trig_out")
        roped = sem("roped")
        qi_padded = sem("qi_padded")
        scored = sem("scored")
        X_ready = sem("X_ready")
        exp_ready = sem("exp_ready")
        P_ready = sem("P_ready")
        mixer1_done = sem("mixer1_done")
        out_hi_ready = [sem("mix_hi_ready"), sem("attn_hi_ready")]
        attn_lo_ready = sem("attn_lo_ready")
        w_hi_ready = sem("w_hi_ready")
        w_lo_ready = sem("w_lo_ready")
        quarter_used = sem("quarter_used")
        M = []
        for lay in range(2):
            s = {name: sem(f"{name}_{lay}") for name in (
                "gate0_used", "gate_full", "up0_used", "up_full", "down0_used", "y_full", "silu_ready",
                "h_ready", "hT_full", "hT_ready", "xc_full", "xc_drained", "y_ready", "sc_full",
                "sc_drained", "pick_ready", "pw_ready")}
            s["loaded"] = [sem(f"expert_unit_loaded_{lay}_{i}") for i in range(6)]
            M.append(s)
        block = ctx.enter_context(nc.Block())

        def filled(stage, i=0):
            return first[stage] + i + 1

        def tile(stage, i=0):
            return ps[(first[stage] + i) % 8]

        def drained_before(eng, stage, i=0):
            t = first[stage] + i - 8
            if t >= 0:
                who = drained_by[t]
                eng.wait_ge(drained[who], drained_by[:t + 1].count(who))

        def all_drained(eng, stage):
            for who in "AD":
                eng.wait_ge(drained[who], drained_by[:first[stage]].count(who))

        w_in = [a["ab_w_in"][0], a["c_w_in"][0]]
        w_out = [a["ab_w_out"][0], a["c_w_out"][0]]
        chunks = [L0_CHUNKS, L1_CHUNKS]

        def chunk_source(lay, c, u):
            n_in = len(chunks[lay])
            w, col = (w_in[lay], chunks[lay][c]) if c < n_in else (w_out[lay], OUT_CHUNKS[c - n_in])
            return w.rearrange("(k p) n -> p k n", p=P)[:, 8 * u:8 * u + 8, col:col + 512]

        def chunk_stage(lay, c):
            n_in = len(chunks[lay])
            if c < n_in:
                return f"chunk{lay}_{c}", (3 if lay == 0 and c < 4 else 1)
            return f"out{lay}", 2 * (c - n_in) + 1

        def wait_quarter_used(eng, lay, q):
            if q % 4 == 3:
                eng.wait_ge(psum_full, filled(f"out{lay}", 2 * (q // 4) + 1))
            else:
                eng.wait_ge(quarter_used, 12 * lay + 3 * (q // 4) + q % 4 + 1)

        def weight_quarter(lay, q):
            n = 2 * len(chunks[lay]) + q // 2
            at = (n % 3) * SLOT + (q % 2) * (SLOT // 2)
            return n, ring[:, at:at + SLOT // 2], w_lo[:, at:at + SLOT // 2]

        gate_w = a["moe_w_gate"].rearrange("l e (p k) n -> l e p (k n)", k=KT)
        up_w = a["moe_w_up"].rearrange("l e (p k) n -> l e p (k n)", k=KT)
        down_w = a["moe_w_down"].rearrange("l e (g p j) n -> l e g p (j n)", g=2, j=2)

        @block.sync
        def _(sp):
            xr = a["x"][0].rearrange("(t p) d -> p t d", p=P)
            for tt in range(TT):
                sp.dma_start(h[:, tt, :], xr[:, tt, :]).then_inc(x_loaded, 16)
            with nc.allow_non_contiguous_dma(reason="columns of the gates, once"):
                wr = w_in[0].rearrange("(k p) n -> p k n", p=P)
                sp.dma_start(w_small0[:, :, 0:8], wr[:, :, MI:MI + 8]).then_inc(small_loaded, 16)
                sp.dma_start(w_small0[:, :, 8:24], wr[:, :, GLR:GLR + RANK]).then_inc(small_loaded, 16)
                sp.dma_start(gate_bias[0:NH, :], a["ab_igate_b"].rearrange("a h -> h a")).then_inc(small_loaded, 16)
                sp.dma_start(gate_bias[32:32 + NH, :], a["ab_fgate_b"].rearrange("a h -> h a")).then_inc(small_loaded, 16)
                sp.dma_start(pos_int[:, :], a["positions"].rearrange("a (t p) -> p (a t)", p=P)).then_inc(small_loaded, 16)
            sp.dma_start(small_rows[0:TAPS * 8, :], a["ab_conv_w"].rearrange("a t (j p) -> (a t j) p", p=P)).then_inc(small_loaded, 16)
            sp.dma_start(small_rows[TAPS * 8:TAPS * 8 + 4, :], a["ab_gla_gate_b"].rearrange("a (j p) -> (a j) p", p=P)).then_inc(small_loaded, 16)
            sp.dma_start(w2[0:RANK, :], a["ab_gla_gate_w2"][0]).then_inc(small_loaded, 16)
            sp.dma_start(router_w[:, :, :], a["router_w"].rearrange("(k p) e -> p k e", p=P)).then_inc(small_loaded, 16)
            sp.dma_start(router_b[:, :], a["router_bias"].partition_broadcast(P)).then_inc(small_loaded, 16)
            sp.dma_start(norm_g[:, 0:1024], a["ab_mlstm_norm_g"][0].partition_broadcast(P)).then_inc(small_loaded, 16)
            sp.dma_start(norm_g[:, 1024:2048], a["ab_gla_norm_g"][0].partition_broadcast(P)).then_inc(small_loaded, 16)

            def load_unit(lay, n):
                if n >= 3:
                    pc, pu = (n - 3) // 2, (n - 3) % 2
                    if pu == 1:
                        sp.wait_ge(psum_full, filled(*chunk_stage(lay, pc)))
                    elif pc >= len(chunks[lay]):
                        wait_quarter_used(sp, lay, 4 * (pc - len(chunks[lay])) + 1)
                    else:
                        sp.wait_ge(half_used[lay], pc + 1)
                elif lay == 1:
                    wait_last_expert(n)
                sp.dma_start(slot(n % 3).rearrange("p (k n) -> p k n", k=8), chunk_source(lay, n // 2, n % 2))\
                  .then_inc(unit_loaded[lay][n % 3], 16)

            order = [3, 4, 5, 0, 1, 2]
            used = ["gate0_used", "gate_full", "up0_used", "up_full", "down0_used", "y_full"]

            def expert_source(lay, e, i):
                if i < 4:
                    w = gate_w if i < 2 else up_w
                    v = w[lay, e] if isinstance(e, int) else w[lay, bass.ds(e, 1)][0]
                    return v[:, (i % 2) * SLOT:(i % 2 + 1) * SLOT]
                v = down_w[lay, e] if isinstance(e, int) else down_w[lay, bass.ds(e, 1)][0]
                return v[i - 4]

            def load_expert(lay, e, x, units):
                for i in units:
                    if not (isinstance(x, int) and x == 0):
                        sp.wait_ge(M[lay][used[i]], x)
                    sp.dma_start(slot(order[i]), expert_source(lay, e, i)).then_inc(M[lay]["loaded"][i], 16)

            def wait_last_expert(s):
                sp.wait_ge(M[0][used[s + 3]], NE * n_rounds[0])

            n_rounds = [None, None]
            for lay in range(2):
                units = 2 * (len(chunks[lay]) + 4)
                for n in range(units - 5):
                    load_unit(lay, n)
                    if lay == 1 and n == 1:
                        sp.wait_ge(M[0]["up_full"], NE * n_rounds[0])
                        with nc.allow_non_contiguous_dma(reason="80 columns, once"):
                            sp.dma_start(w_small1[:, :, :], w_in[1].rearrange("(k p) n -> p k n", p=P)[:, :, KI:KI + 80])\
                              .then_inc(small1_loaded, 16)
                sp.wait_ge(mix_ready if lay == 0 else mixer1_done, 1)
                for i in range(5):
                    if i < 3:
                        load_expert(lay, 0, 0, [i])
                    load_unit(lay, units - 5 + i)
                sp.wait_ge(psum_full, filled(f"out{lay}", 7))
                load_expert(lay, 0, 0, [3, 4, 5])
                with sp.Fori(1, NE) as e:
                    load_expert(lay, e, e, range(6))
                sp.wait_ge(routed, lay + 1)
                n_rounds[lay] = sp.value_load(rounds_i[0:1, 0:1], min_val=0, max_val=MAX_ROUNDS - 1) + 1
                with sp.If(n_rounds[lay] > 1):
                    with sp.Fori(1, n_rounds[lay]) as r:
                        with sp.Fori(0, NE) as e:
                            load_expert(lay, e, r * NE + e, range(6))
            for tt in range(TT):
                sp.wait_ge(h_ready, 3 * TT + tt + 1)
                sp.dma_start(out[0].rearrange("(t p) d -> p t d", p=P)[:, tt, :], h[:, tt, :]).then_inc(out_stored, 16)
            sp.wait_ge(out_stored, 16 * TT)

        @block.gpsimd
        def _(pool):
            step = [0]

            def link(ins):
                step[0] += 1
                ins.then_inc(pool_step, 1)
                pool.wait_ge(pool_step, step[0])

            pool.memset(ident[:, :], 0.0)
            pool.memset(maskT[:, :], 0.0)
            pool.memset(maskN[:, :], 0.0)
            pool.memset(before[:, :], 0.0)
            pool.memset(ones[:, :], 1.0)
            pool.memset(mhalf[:, :], -0.5)
            pool.memset(pick[0:NH, :, :], 0.0)
            pool.memset(resets[:, :], 1.0)
            pool.memset(V[:, :, :, DV:DV + 1], 1.0)
            link(pool.memset(cmf[:, :], 0.0))
            pool.affine_select(out=ident[:, :], in_=ident[:, :], compare_op=ALU.not_equal, fill=1.0, base=0,
                               pattern=[[-1, P]], channel_multiplier=1)
            pool.affine_select(out=maskT[:, 0:P], in_=maskT[:, 0:P], compare_op=ALU.is_ge, fill=NEG, base=0,
                               pattern=[[1, P]], channel_multiplier=-1)
            pool.affine_select(out=maskN[:, P:2 * P], in_=maskN[:, P:2 * P], compare_op=ALU.is_ge, fill=NEG, base=0,
                               pattern=[[-1, P]], channel_multiplier=1)
            pool.affine_select(out=before[:, :], in_=before[:, :], compare_op=ALU.is_ge, fill=1.0, base=0,
                               pattern=[[-1, P]], channel_multiplier=1)
            pool.affine_select(out=pick[0:NH, :, :], in_=pick[0:NH, :, :], compare_op=ALU.not_equal, fill=1.0, base=0,
                               pattern=[[-1, NH], [0, P]], channel_multiplier=1)
            link(pool.memset(resets[:, :].rearrange("p (a b) -> p a b", b=CH)[:, :, 0:1], 0.0))
            link(pool.affine_select(out=cmf[:, :], in_=cmf[:, :], compare_op=ALU.is_gt, fill=1.0, base=0,
                                    pattern=[[-1, P]], channel_multiplier=1))
            link(pool.memset(cmf[0:CH, CH:P], 0.0))
            link(pool.tensor_copy(chunk_mask, cmf[:, :]))
            link(pool.iota(slots64[:, :], pattern=[[1, CAP]], base=0, channel_multiplier=0,
                           allow_small_or_imprecise_dtypes=True))
            pool.memset(mhalf[:, 0:1], -0.5).then_inc(consts_ready, 1)

            def load_ln(g, b):
                pool.dma_start(ln_gb[:, 0, :], g.partition_broadcast(P)).then_inc(ln_loaded, 16)
                pool.dma_start(ln_gb[:, 1, :], b.partition_broadcast(P)).then_inc(ln_loaded, 16)

            def rstd_step(n):
                pool.wait_ge(var_ready, n + 1)
                pool.tensor_tensor(rstd[:, :], var_eps[:, :], mhalf[:, 0:TT], ALU.pow).then_inc(rstd_ready, 1)

            for lay in range(2):
                if lay == 0:
                    for br in range(2):
                        pool.wait_ge(ssq_scaled, br + 1)
                        sl = slice(br * TT * NH, (br + 1) * TT * NH)
                        pool.tensor_tensor(hn_r[:, sl], ssq_m[:, sl], mhalf[:, 0:TT * NH], ALU.pow).then_inc(hr_ready, 1)
                    pool.wait_ge(mix_ready, 1)
                else:
                    pool.wait_ge(mixer1_done, 1)
                load_ln(a["ln_mix_g"][lay], a["ln_mix_b"][lay])
                rstd_step(2 * lay)
                pool.wait_ge(h_ready, TT * (2 * lay + 1))
                load_ln(a["ln_ffn_g"][lay], a["ln_ffn_b"][lay])
                rstd_step(2 * lay + 1)
                if lay == 0:
                    pool.wait_ge(h_ready, 2 * TT)
                    pool.memset(qiT[IDH:P, :, :], 0.0).then_inc(qi_padded, 1)

        @block.tensor
        def _(pe):
            def transposes(stage, i, sources, identity=None):
                drained_before(pe, stage, i)
                t = tile(stage, i)
                for n, src in enumerate(sources):
                    k = src.shape[0]
                    m = src.shape[1]
                    last = nc.tensor.transpose(t[0:m, n * P:n * P + k], src, ident[0:k, 0:k])
                last.then_inc(psum_full, 1)

            def transpose_hidden(stage, src, ready=None, count=0):
                for i in range(8):
                    tt, k0 = i // 4, 4 * (i % 4)
                    if ready is not None and i % 4 == 0:
                        pe.wait_ge(ready, count + tt)
                    transposes(stage, i, [src[:, tt, (k0 + k) * P:(k0 + k + 1) * P] for k in range(4)])

            def wait_hT(stage):
                t = first[stage] + 7
                for who in "AD":
                    pe.wait_ge(drained[who], drained_by[:t + 1].count(who))

            def wait_unit(lay, n):
                pe.wait_ge(unit_loaded[lay][n % 3], 16 * (n // 3 + 1))

            def chunk_transposed(lay, c):
                stage = f"chunk{lay}_{c}"
                for u in range(2):
                    wait_unit(lay, 2 * c + u)
                    w = slot((2 * c + u) % 3).rearrange("p (k n) -> p k n", k=8)
                    for j in range(4):
                        if u == 0:
                            drained_before(pe, stage, j)
                        for k in range(8):
                            last = nc.tensor.matmul(tile(stage, j)[:, 0:SEQ], w[:, k, j * P:(j + 1) * P], hT[:, 8 * u + k, :],
                                                    start=(u + k == 0), stop=(u == 1 and k == 7))
                        if u == 1:
                            last.then_inc(psum_full, 1)
                    if u == 0:
                        last.then_inc(half_used[lay], 1)

            def chunk_natural(lay, c):
                stage, lt = chunk_stage(lay, c)
                for u in range(2):
                    wait_unit(lay, 2 * c + u)
                    w = slot((2 * c + u) % 3).rearrange("p (k n) -> p k n", k=8)
                    for tt in range(TT):
                        i = lt - 1 + tt
                        if u == 0:
                            drained_before(pe, stage, i)
                        for k in range(8):
                            last = nc.tensor.matmul(tile(stage, i)[:, :], hT[:, 8 * u + k, tt * P:(tt + 1) * P], w[:, k, :],
                                                    start=(u + k == 0), stop=(u == 1 and k == 7))
                        if u == 1:
                            last.then_inc(psum_full, 1)
                    if u == 0:
                        last.then_inc(half_used[lay], 1)

            def out_chunk(lay, c):
                stage = f"out{lay}"
                for part in range(4):
                    q = 4 * c + part
                    pe.wait_ge(w_lo_ready, 16 * lay + q + 1)
                    w_l = weight_quarter(lay, q)[2].rearrange("p (k n) -> p k n", k=4)
                    w_h = w_hi[:, q % 2, :].rearrange("p (k n) -> p k n", k=4)
                    for tt in range(TT):
                        if part == 0:
                            drained_before(pe, stage, 2 * c + tt)
                        t = tile(stage, 2 * c + tt)[:, :]
                        for k in range(4):
                            x_h = x_hi[:, 4 * part + k, tt * P:(tt + 1) * P]
                            x_l = x_lo[:, 4 * part + k, tt * P:(tt + 1) * P]
                            nc.tensor.matmul(t, x_h, w_l[:, k, :], start=(part + k == 0), stop=False)
                            nc.tensor.matmul(t, x_h, w_h[:, k, :], start=False, stop=False)
                            last = nc.tensor.matmul(t, x_l, w_h[:, k, :], start=False, stop=(part + k == 6))
                        if part == 3:
                            last.then_inc(psum_full, 1)
                    if part < 3:
                        last.then_inc(quarter_used, 1)

            def mlstm_scores(hd):
                stage = f"mS{hd}"
                drained_before(pe, stage, 0)
                pe.wait_ge(rows_done, 1)
                nc.tensor.matmul(tile(stage, 0)[:, 0:SEQ], pick[0:NH, hd, :], row["nM"], start=True, stop=True).then_inc(psum_full, 1)
                drained_before(pe, stage, 1)
                pe.wait_ge(qk_silu, 8)
                t = tile(stage, 1)
                nc.tensor.matmul(t[:, 0:SEQ], QKT[:, 4 + hd, 0:P], QKT[:, hd, :], start=True, stop=True)
                nc.tensor.matmul(t[:, SEQ:SEQ + P], QKT[:, 4 + hd, P:2 * P], QKT[:, hd, P:2 * P], start=True, stop=True).then_inc(psum_full, 1)

            def mlstm_out(hd):
                stage = f"mO{hd}"
                w = W[:, hd % 2, :]
                pe.wait_ge(W_ready, hd + 1)
                drained_before(pe, stage, 0)
                nc.tensor.matmul(tile(stage, 0)[:, 0:DV + 1], w[:, 0:P], V[:, 0, hd, :], start=True, stop=True).then_inc(psum_full, 1)
                drained_before(pe, stage, 1)
                nc.tensor.matmul(tile(stage, 1)[:, 0:DV + 1], w[:, P:2 * P], V[:, 0, hd, :], start=True, stop=False)
                nc.tensor.matmul(tile(stage, 1)[:, 0:DV + 1], w[:, 2 * P:3 * P], V[:, 1, hd, :], start=False, stop=True).then_inc(psum_full, 1)

            def wait_values(stage):
                t = first[stage] + 1
                pe.wait_ge(drained["A"], drained_by[:t + 1].count("A"))

            pe.wait_ge(consts_ready, 1)
            pe.wait_ge(x_loaded, 16 * TT)
            transpose_hidden("xT0", h)
            pe.wait_ge(small_loaded, 16 * 12)
            transposes("rows", 0, [small_rows[:, :]])
            wait_hT("xT0")
            drained_before(pe, "gates", 0)
            for k in range(KT):
                for at, lo, hi in ((0, 0, NH), (32, NH, 2 * NH), (64, 8, 8 + RANK)):
                    last = nc.tensor.matmul(tile("gates")[at:at + hi - lo, 0:SEQ], w_small0[:, k, lo:hi], hT[:, k, :],
                                            start=(k == 0), stop=(k == KT - 1), skip_group_check=True)
            last.then_inc(psum_full, 1)
            for c in range(4):
                chunk_transposed(0, c)
            pe.wait_ge(drained["D"], drained_by[:first["gates"] + 1].count("D"))
            for i in range(2):
                drained_before(pe, "decay", i)
                for j in range(2):
                    hd = 2 * i + j
                    last = nc.tensor.matmul(tile("decay", i)[:, j * SEQ:(j + 1) * SEQ], w2[0:RANK, hd * DK:(hd + 1) * DK],
                                            t3[0:RANK, 0:SEQ], start=True, stop=True)
                last.then_inc(psum_full, 1)
            pe.wait_ge(e_done, 1)
            pe.wait_ge(rows_done, 1)
            transposes("gcols", 0, [row["g"][:, 0:P], row["g"][:, P:2 * P], row["e"][:, 0:P], row["e"][:, P:2 * P]])
            chunk_natural(0, 4)
            chunk_natural(0, 5)
            chunk_natural(0, 6)
            mlstm_scores(0)
            for hd in range(1, NH):
                chunk_natural(0, 6 + hd)
                if hd == 1:
                    wait_values("chunk0_5")
                mlstm_out(hd - 1)
                mlstm_scores(hd)
            pe.wait_ge(kend_done, 1)
            for tt in range(TT):
                transposes("kend", tt, [t3[:, hd * SEQ + tt * P:hd * SEQ + (tt + 1) * P] for hd in range(NH)])
            mlstm_out(NH - 1)
            chunk_natural(0, 10)
            wait_values("chunk0_9")
            t = first["kend"] + 1
            pe.wait_ge(drained["A"], drained_by[:t + 1].count("A"))
            for c in range(3):
                for hp in range(2):
                    i = 2 * c + hp
                    drained_before(pe, "gstate", i)
                    for j in range(2):
                        hd = 2 * hp + j
                        last = nc.tensor.matmul(tile("gstate", i)[:, j * DV:(j + 1) * DV], kz[:, (c // 2) * NH + hd, c % 2, :],
                                                V[:, c // 2, NH + hd, 0:DV], start=True, stop=True)
                    last.then_inc(psum_full, 1)
            pe.wait_ge(qdec_done, 2)
            for tt in range(TT):
                drained_before(pe, "gattn", tt)
                for hd in range(NH):
                    last = nc.tensor.matmul(tile("gattn", tt)[:, hd * P:(hd + 1) * P], QKT[:, 12 + hd, tt * P:(tt + 1) * P],
                                            QKT[:, 8 + hd, tt * P:(tt + 1) * P], start=True, stop=True)
                last.then_inc(psum_full, 1)
            pe.wait_ge(attn_ready, TT)
            for tt in range(TT):
                pe.wait_ge(state_ready, 6 if tt else 2)
                for hp in range(2):
                    i = 2 * tt + hp
                    drained_before(pe, "gO", i)
                    for j in range(2):
                        hd = 2 * hp + j
                        o_t = tile("gO", i)[:, j * DV:(j + 1) * DV]
                        nc.tensor.matmul(o_t, attnT[:, tt * NH + hd, :], V[:, tt, NH + hd, 0:DV], start=True, stop=False,
                                         skip_group_check=True)
                        for c in ([1] if tt == 0 else [2, 3]):
                            r0 = (c % 2) * CH
                            last = nc.tensor.matmul(tile("gO", i)[r0:r0 + CH, j * DV:(j + 1) * DV],
                                                    QKT[:, 8 + hd, c * CH:(c + 1) * CH], state[:, c - 1, hd, :],
                                                    start=False, stop=True, skip_group_check=True)
                    last.then_inc(psum_full, 1)
            chunk_natural(0, 11)
            pe.wait_ge(mix_ready, 1)
            transpose_hidden("mixT0", mix)
            wait_hT("mixT0")
            for c in range(4):
                out_chunk(0, c)

            def experts(lay):
                s = M[lay]
                transpose_hidden(f"moeT{lay}", h, h_ready, TT * 2 * lay + 1)
                wait_hT(f"moeT{lay}")
                drained_before(pe, f"route{lay}", 0)
                for k in range(KT):
                    last = nc.tensor.matmul(tile(f"route{lay}")[0:NE, 0:SEQ], router_w[:, k, :], hT[:, k, :],
                                            start=(k == 0), stop=(k == KT - 1))
                last.then_inc(psum_full, 1)
                drained_before(pe, f"route{lay}", 1)
                pe.wait_ge(drained["D"], drained_by[:first[f"route{lay}"] + 1].count("D"))
                for tt in range(TT):
                    last = nc.tensor.transpose(tile(f"route{lay}", 1)[:, tt * NE:(tt + 1) * NE], logits_T[0:NE, tt * P:(tt + 1) * P],
                                               ident[0:NE, 0:NE])
                last.then_inc(psum_full, 1)
                pe.wait_ge(mask_ready, lay + 1)
                drained_before(pe, f"pos{lay}", 0)
                t = tile(f"pos{lay}")
                nc.tensor.matmul(t[:, 0:NE], before[:, :], chosen[:, 0, :], start=True, stop=True)
                nc.tensor.matmul(t[:, NE:2 * NE], ones[:, :], chosen[:, 0, :], start=True, stop=False)
                nc.tensor.matmul(t[:, NE:2 * NE], before[:, :], chosen[:, 1, :], start=False, stop=True)
                nc.tensor.matmul(t[:, 2 * NE:3 * NE], ones[:, :], chosen[:, 0, :], start=True, stop=False)
                nc.tensor.matmul(t[:, 2 * NE:3 * NE], ones[:, :], chosen[:, 1, :], start=False, stop=True).then_inc(psum_full, 1)
                pe.wait_ge(routed, lay + 1)
                n_r = pe.value_load(rounds_i[0:1, 0:1], min_val=0, max_val=MAX_ROUNDS - 1) + 1

                def gather(tiles_before, pair):
                    pe.wait_ge(s["pick_ready"], pair + 1)
                    for g in range(4):
                        bank = ps[4 + g % 2]
                        if not (isinstance(tiles_before, int) and tiles_before + g < 2):
                            pe.wait_ge(s["xc_drained"], tiles_before + g - 1)
                        for k in range(4):
                            for tt in range(TT):
                                last = nc.tensor.matmul(bank[:, k * P:(k + 1) * P], h[:, tt, 4 * g + k::KT], pick_p[:, tt, :],
                                                        start=(tt == 0), stop=(tt == TT - 1))
                        last.then_inc(s["xc_full"], 1)

                def scatter_tile(x, t8):
                    c, tt = t8 // 2, t8 % 2
                    if not (isinstance(x, int) and x == 0 and t8 < 2):
                        pe.wait_ge(s["sc_drained"], 8 * x + t8 - 1)
                    nc.tensor.matmul(ps[6 + t8 % 2][:, :], pw_T[:, c // 2, tt, :], y_sb[:, (c % 2) * BANK:(c % 2 + 1) * BANK],
                                     start=True, stop=True).then_inc(s["sc_full"], 1)

                def expert(q, i, is_first, is_last):
                    x = 2 * q + i
                    begun = not (is_first and i == 0)
                    units = [slot(n) for n in (3, 4, 5, 0, 1, 2)]
                    if i == 0:
                        pe.wait_ge(s["xc_drained"], 6 * q + 4)
                    for part in range(4):
                        pe.wait_ge(s["loaded"][part], 16 * (x + 1))
                        w = units[part].rearrange("p (k n) -> p k n", k=8)
                        for k in range(8):
                            kt = 8 * (part % 2) + k
                            for hf in range(2):
                                last = nc.tensor.matmul(ps[part // 2][hf * CAP:(hf + 1) * CAP, 0:DV],
                                                        xcT[:, kt, i * CAP:(i + 1) * CAP], w[:, k, hf * DV:(hf + 1) * DV],
                                                        start=(kt == 0), stop=(kt == KT - 1), skip_group_check=True)
                        last.then_inc(s[("gate0_used", "gate_full", "up0_used", "up_full")[part]], 1)
                    if begun:
                        pe.wait_ge(s["y_ready"], x)
                        pe.wait_ge(s["xc_drained"], (6 * q + 4) if i == 0 else (6 * q + 5))
                        for t8 in range(6):
                            scatter_tile(x - 1, t8)
                    pe.wait_ge(s["h_ready"], x + 1)
                    for j in range(2):
                        last = nc.tensor.transpose(ps[0][:, j * P:(j + 1) * P], h_e[:, j::2], ident[:, :])
                    last.then_inc(s["hT_full"], 1)
                    if begun:
                        for t8 in range(6, 8):
                            scatter_tile(x - 1, t8)
                    pe.wait_ge(s["pw_ready"], x + 1)
                    pe.wait_ge(s["xc_drained"], 6 * q + 3 + i)
                    for ab in range(2):
                        for tt in range(TT):
                            last = nc.tensor.transpose(ps[4 + i][:, (ab * TT + tt) * P:(ab * TT + tt + 1) * P],
                                                       pick_w[:, i, tt, CAP * (1 - ab):CAP * (1 - ab) + P], ident[:, :])
                    last.then_inc(s["xc_full"], 1)
                    if i == 1 and not is_last:
                        gather(6 * q + 6, q + 1)
                    pe.wait_ge(s["hT_ready"], x + 1)
                    if begun:
                        pe.wait_ge(s["y_ready"], x)
                    for hf in range(2):
                        pe.wait_ge(s["loaded"][4 + hf], 16 * (x + 1))
                        w = units[4 + hf].rearrange("p (j n) -> p j n", j=2)
                        for j in range(2):
                            for cc in range(2):
                                for side in range(2):
                                    col = side * 2 * BANK + cc * BANK
                                    last = nc.tensor.matmul(ps[2 + cc][side * CAP:(side + 1) * CAP, :],
                                                            hT_e[:, j, hf * CAP:(hf + 1) * CAP], w[:, j, col:col + BANK],
                                                            start=(hf + j == 0), stop=(hf + j == 2), skip_group_check=True)
                        last.then_inc(s["y_full" if hf else "down0_used"], 1)

                all_drained(pe, f"xT{lay + 1}" if lay == 0 else f"pos{lay}")
                gather(0, 0)
                for i in range(2):
                    expert(0, i, True, False)
                n_pairs = n_r * PAIRS
                with pe.Fori(1, n_pairs - 1) as q:
                    for i in range(2):
                        expert(q, i, False, False)
                q = n_pairs - 1
                for i in range(2):
                    expert(q, i, False, True)
                pe.wait_ge(s["y_ready"], 2 * n_pairs)
                pe.wait_ge(s["xc_drained"], 6 * q + 6)
                for t8 in range(8):
                    scatter_tile(2 * q + 1, t8)
                pe.wait_ge(s["sc_drained"], 16 * n_pairs)

            experts(0)

            transpose_hidden("xT1", h, h_ready, TT + 1)
            wait_hT("xT1")
            drained_before(pe, "small1", 0)
            pe.wait_ge(small1_loaded, 16)
            for k in range(KT):
                last = nc.tensor.matmul(tile("small1")[0:IDH + IH, 0:SEQ], w_small1[:, k, :], hT[:, k, :],
                                        start=(k == 0), stop=(k == KT - 1))
            last.then_inc(psum_full, 1)

            def wait_tiles(stage, n):
                t = first[stage] + n
                for who in "AD":
                    pe.wait_ge(drained[who], drained_by[:t].count(who))

            chunk_natural(1, 0)
            pe.wait_ge(drained["D"], drained_by[:first["small1"] + 1].count("D"))
            drained_before(pe, "small1T")
            for tt in range(TT):
                last = nc.tensor.transpose(tile("small1T")[:, tt * P:tt * P + IDH + IH], small_T[:, tt * P:(tt + 1) * P],
                                           ident[0:IDH + IH, 0:IDH + IH])
            last.then_inc(psum_full, 1)
            for c in (1, 2):
                chunk_natural(1, c)
            pe.wait_ge(roped, 1)
            pe.wait_ge(qi_padded, 1)
            for i in range(9):
                heads = [hd for hd in (2 * i, 2 * i + 1) if hd < IH + 1]
                transposes("qiT", i, [QIN[:, tt, hd, :] for hd in heads for tt in range(TT)])
            wait_tiles("qiT", 9)
            for i in range(12):
                drained_before(pe, "index", i)
                tt, hs, nk = (1, range(2 * i, 2 * i + 2), SEQ) if i < 8 else (0, range(4 * (i - 8), 4 * (i - 8) + 4), P)
                for n, hd in enumerate(hs):
                    last = nc.tensor.matmul(tile("index", i)[:, n * nk:(n + 1) * nk], qiT[:, hd, tt * P:(tt + 1) * P],
                                            qiT[:, IH, 0:nk], start=True, stop=True)
                last.then_inc(psum_full, 1)
            pe.wait_ge(roped, 2)
            for i in range(2):
                transposes("kT", i, [QN[:, tt, AH + 2 * i + j, :] for j in range(2) for tt in range(TT)])
            for c in (3, 4):
                chunk_natural(1, c)

            def heads_in(g):
                pe.wait_ge(roped, 3 + g)
                for i in range(2):
                    transposes(f"qT{g}", i, [QN[:, tt, GQ * g + 2 * i + j, :] for j in range(2) for tt in range(TT)])
                wait_tiles(f"qT{g}", 2)
                for tt in range(TT):
                    nk = P * (tt + 1)
                    per = BANK // nk
                    for i in range(GQ // per):
                        drained_before(pe, f"S{tt}_{g}", i)
                        for j in range(per):
                            last = nc.tensor.matmul(tile(f"S{tt}_{g}", i)[:, j * nk:(j + 1) * nk],
                                                    qT[:, GQ * g + per * i + j, tt * P:(tt + 1) * P], qT[:, AH + g, 0:nk],
                                                    start=True, stop=True)
                        last.then_inc(psum_full, 1)

            def heads_out(g):
                for tt in range(TT):
                    pe.wait_ge(P_ready, TT * g + tt + 1)
                    for kt in range(tt + 1):
                        transposes(f"PT{tt}_{g}", kt, [X[g % 2][tt][:, j, kt * P:(kt + 1) * P] for j in range(GQ)])
                    wait_tiles(f"PT{tt}_{g}", tt + 1)
                    drained_before(pe, f"O{tt}_{g}", 0)
                    for kt in range(tt + 1):
                        last = nc.tensor.matmul(tile(f"O{tt}_{g}")[:, :], VN[:, kt, g, :], PT[tt][:, kt, :],
                                                start=(kt == 0), stop=(kt == tt))
                    last.then_inc(psum_full, 1)

            heads_in(0)
            chunk_natural(1, 5)
            heads_in(1)
            chunk_natural(1, V_CHUNK)
            heads_out(0)
            heads_in(2)
            chunk_natural(1, 7)
            heads_out(1)
            heads_in(3)
            heads_out(2)
            heads_out(3)
            pe.wait_ge(attn_lo_ready, KVH)
            for c in range(4):
                out_chunk(1, c)
            experts(1)

        @block.scalar
        def _(act):
            step = [0]

            def link(ins):
                step[0] += 1
                ins.then_inc(act_s, 1)
                act.wait_ge(act_s, step[0])

            def hT_tiles(stage):
                for i in range(0, 8, 2):
                    act.wait_ge(psum_full, filled(stage, i))
                    act.activation(hT[:, 4 * (i % 4):4 * (i % 4) + 4, (i // 4) * P:(i // 4 + 1) * P],
                                   tile(stage, i)[:, :].rearrange("p (a b) -> p a b", a=4), ACT.Copy)\
                       .then_inc(drained["A"], 1)

            def weight_hi(lay, q):
                if q >= 2:
                    wait_quarter_used(act, lay, q - 2)
                n, w, lo = weight_quarter(lay, q)
                act.wait_ge(unit_loaded[lay][n % 3], 16 * (n // 3 + 1))
                act.activation(w_hi[:, q % 2, :], w, ACT.Copy).then_inc(w_hi_ready, 1)

            hT_tiles("xT0")
            act.wait_ge(lf_abs, 1)
            link(act.activation(row["ab"], row["xf"], ACT.Abs))
            link(act.activation(row["ab"], row["ab"], ACT.Exp, scale=-1.0))
            act.activation(row["ab"], row["ab"], ACT.Ln, bias=1.0).then_inc(lf_log, 1)
            act.wait_ge(rows_done, 1)
            act.activation(row["e"], row["m"], ACT.Exp, scale=-1.0).then_inc(e_done, 1)
            for j in range(8):
                act.wait_ge(conv_done, j + 1)
                act.activation(QKT[:, j, :], QKT[:, j, :], ACT.Silu).then_inc(qk_silu, 1)
            for c in (2, 3):
                for j in range(4):
                    act.wait_ge(psum_full, filled(f"chunk0_{c}", j))
                    act.activation(QKT[:, 4 * c + j, :], tile(f"chunk0_{c}", j)[:, 0:SEQ], ACT.Copy,
                                   scale=(DK ** -0.5 if c == 2 else 1.0)).then_inc(drained["A"], 1)
            act.wait_ge(gla_x, 1)
            link(act.activation(t2[:, :], t1[:, :], ACT.Abs))
            link(act.activation(t2[:, :], t2[:, :], ACT.Exp, scale=-1.0))
            act.activation(t2[:, :], t2[:, :], ACT.Ln, bias=1.0).then_inc(gla_log, 1)

            def values(c):
                for tt in range(TT):
                    act.wait_ge(psum_full, filled(f"chunk0_{c}", tt))
                    src = tile(f"chunk0_{c}", tt)[:, :]
                    if c in (4, 5, 8, 9):
                        hd = {4: 0, 5: 2, 8: 4, 9: 6}[c]
                        dst = V[:, tt, hd:hd + 2, 0:DV]
                        src = src.rearrange("p (a b) -> p a b", a=2)
                    else:
                        col = {6: 0, 7: 512, 10: 1024, 11: 1536}[c]
                        dst = mix[:, tt, col:col + 512]
                    ins = act.activation(dst, src, ACT.Copy)
                    ins.then_inc(drained["A"], 1)

            def mlstm_exp(hd):
                act.wait_ge(D_ready, hd + 1)
                act.wait_ge(cols_done, 1)
                w = Dl[:, hd % 2, :]
                act.activation(w[:, 0:SEQ], w[:, 0:SEQ], ACT.Exp, bias=gcol[:, 0, hd:hd + 1])
                act.activation(w[:, SEQ:SEQ + P], w[:, SEQ:SEQ + P], ACT.Exp, bias=gcol[:, 1, hd:hd + 1]).then_inc(E_ready, 1)

            def mlstm_square(hd):
                for tt in range(TT):
                    n = tt * NH + hd
                    act.wait_ge(hn_ready, TT * hd + tt + 1)
                    if hd + tt > 0:
                        act.wait_ge(ssq_ready, TT * hd + tt)
                    act.activation(t2[:, 0:DV], hn[:, n, :], ACT.Square, accum_out=ssq[:, n:n + 1]).then_inc(ssq_ready, 1)

            values(4)
            act.wait_ge(la_done, 1)
            act.activation(t1[:, :], la[:, :], ACT.Exp, scale=1.0 / 16).then_inc(gla_exp, 1)
            act.activation(t2[:, :], la[:, :], ACT.Exp, scale=-1.0 / 16).then_inc(gla_exp, 1)
            act.activation(decay[:, :], la_last[:, :], ACT.Exp)
            for n in range(NH * 4):
                sl = slice(n * CH, (n + 1) * CH)
                last = act.activation(t3[:, sl], la[:, sl], ACT.Exp, bias=la_last[:, n:n + 1], scale=-1.0 / 16)
            last.then_inc(gla_exp, 1)
            values(5)
            values(6)
            mlstm_exp(0)
            for hd in range(1, NH):
                values(6 + hd)
                if hd == 1:
                    act.wait_ge(qdec_done, 2)
                mlstm_square(hd - 1)
                mlstm_exp(hd)
            mlstm_square(NH - 1)
            act.wait_ge(kz_zero, 1)
            for tt in range(TT):
                act.wait_ge(psum_full, filled("kend", tt))
                src = tile("kend", tt)[:, :].rearrange("p (h d) -> p h d", h=NH)
                act.activation(kz[0:CH, tt * NH:(tt + 1) * NH, 0, :], src[0:CH], ACT.Copy)
                act.activation(kz[CH:P, tt * NH:(tt + 1) * NH, 1, :], src[CH:P], ACT.Copy).then_inc(drained["A"], 1)
            values(10)
            t = first["chunk0_10"] + 1
            act.wait_ge(drained["A"], drained_by[:t + 1].count("A"))
            act.activation(mix[:, :, 0:1024], mix[:, :, 0:1024], ACT.Sigmoid).then_inc(gates_done, 1)
            act.activation(mix[:, :, 1024:1536], mix[:, :, 1024:1536], ACT.Silu).then_inc(gates_done, 1)
            act.wait_ge(mlstm_mixed, 1)
            for i in range(4):
                tt, hp = i // 2, i % 2
                act.wait_ge(psum_full, filled("gO", i))
                for j in range(2):
                    n = tt * NH + 2 * hp + j
                    src = tile("gO", i)[:, j * DV:(j + 1) * DV]
                    act.activation(hn[:, n, :], src, ACT.Copy).then_inc(hn_ready, 1)
                    if j == 0:
                        act.wait_ge(ssq_ready, TT * NH + i)
                        if i:
                            act.wait_ge(drained["A"], drained_by[:first["gO"] + i].count("A"))
                    last = act.activation(t2[:, j * DV:(j + 1) * DV], src, ACT.Square, accum_out=ssq[:, TT * NH + n:TT * NH + n + 1])
                    if j == 0:
                        last.then_inc(ssq_ready, 1)
                    else:
                        last.then_inc(drained["A"], 1)
            act.wait_ge(psum_full, filled("gO", 3))
            for q in range(2):
                weight_hi(0, q)
            values(11)
            t = first["chunk0_11"] + 1
            act.wait_ge(drained["A"], drained_by[:t + 1].count("A"))
            act.activation(mix[:, :, 1536:2048], mix[:, :, 1536:2048], ACT.Silu).then_inc(gates_done, 1)
            for i in range(8):
                act.wait_ge(psum_full, filled("mixT0", i))
                act.activation(x_hi[:, 4 * (i % 4):4 * (i % 4) + 4, (i // 4) * P:(i // 4 + 1) * P],
                               tile("mixT0", i)[:, :].rearrange("p (a b) -> p a b", a=4), ACT.Copy)\
                   .then_inc(out_hi_ready[0], 1)
            for q in range(2, 16):
                weight_hi(0, q)

            def experts(lay):
                s = M[lay]
                hT_tiles(f"moeT{lay}")
                act.wait_ge(logits_ready, lay + 1)
                act.activation(aff[:, :, :], aff[:, :, :], ACT.Sigmoid).then_inc(aff_ready, 1)
                act.wait_ge(routed, lay + 1)
                n_r = act.value_load(rounds_i[0:1, 0:1], min_val=0, max_val=MAX_ROUNDS - 1) + 1

                def gathered(tiles_before):
                    for g in range(4):
                        act.wait_ge(s["xc_full"], tiles_before + g + 1)
                        act.activation(xcT[:, 4 * g:4 * g + 4, :].rearrange("p a b -> p (a b)"), ps[4 + g % 2][:, :], ACT.Copy)\
                           .then_inc(s["xc_drained"], 1)

                def expert(q, i, is_first, is_last):
                    x = 2 * q + i
                    begun = not (is_first and i == 0)
                    act.wait_ge(s["gate_full"], x + 1)
                    if begun:
                        act.wait_ge(s["h_ready"], x)
                    act.activation(silu_g[:, :], ps[0][:, 0:DV], ACT.Silu).then_inc(s["silu_ready"], 1)
                    act.wait_ge(s["hT_full"], x + 1)
                    if begun:
                        act.wait_ge(s["y_full"], x)
                    act.activation(hT_e[:, :, :].rearrange("p a b -> p (a b)"), ps[0][:, 0:2 * P], ACT.Copy)\
                       .then_inc(s["hT_ready"], 1)
                    act.wait_ge(s["xc_full"], 6 * q + 5 + i)
                    if begun:
                        act.wait_ge(s["sc_full"], 8 * x)
                    act.activation(pw_T[:, :, :, :].rearrange("p a b c -> p (a b c)"), ps[4 + i][:, :], ACT.Copy)\
                       .then_inc(s["xc_drained"], 1)
                    if i == 1 and not is_last:
                        gathered(6 * q + 6)
                    act.wait_ge(s["y_full"], x + 1)
                    act.activation(y_sb[:, 0:BANK], ps[2][:, :], ACT.Copy)
                    act.activation(y_sb[:, BANK:2 * BANK], ps[3][:, :], ACT.Copy).then_inc(s["y_ready"], 1)

                gathered(0)
                for i in range(2):
                    expert(0, i, True, False)
                with act.Fori(1, n_r * PAIRS - 1) as q:
                    for i in range(2):
                        expert(q, i, False, False)
                for i in range(2):
                    expert(n_r * PAIRS - 1, i, False, True)

            experts(0)

            hT_tiles("xT1")
            act.wait_ge(trig_in, 1)
            act.activation(sinv[:, :, :].rearrange("p a b -> p (a b)"), kf[:, 0, :], ACT.Sin)
            act.activation(cosv[:, :, :].rearrange("p a b -> p (a b)"), kf[:, 1, :], ACT.Sin).then_inc(trig_out, 1)

            def projected(c):
                for tt in range(TT):
                    act.wait_ge(psum_full, filled(f"chunk1_{c}", tt))
                    if c < 2:
                        dst = QIN[:, tt, 8 * c:8 * c + 8, :]
                    elif c == 2:
                        dst = QN[:, tt, AH:AH + KVH, :]
                    elif c == V_CHUNK:
                        dst = VN[:, tt, :, :]
                    else:
                        g = Q_CHUNK.index(c)
                        dst = QN[:, tt, GQ * g:GQ * (g + 1), :]
                    act.activation(dst.rearrange("p a b -> p (a b)"), tile(f"chunk1_{c}", tt)[:, :], ACT.Copy)\
                       .then_inc(drained["A"], 1)

            def heads_in(g):
                act.wait_ge(psum_full, filled(f"qT{g}", 0))
                act.activation(qT[:, GQ * g:GQ * g + 2, :].rearrange("p a b -> p (a b)"), tile(f"qT{g}", 0)[:, :], ACT.Copy)\
                   .then_inc(drained["A"], 1)
                for tt in range(TT):
                    act.wait_ge(X_ready, TT * g + tt + 1)
                    for j in range(GQ):
                        x = X[g % 2][tt][:, j, :]
                        last = act.activation(x, x, ACT.Exp, bias=mx[:, tt, GQ + j:GQ + j + 1],
                                              accum_out=mx[:, tt, 2 * GQ + j:2 * GQ + j + 1])
                    last.then_inc(exp_ready, 1)

            def heads_out(g):
                for tt in range(TT):
                    for kt in range(tt + 1):
                        act.wait_ge(psum_full, filled(f"PT{tt}_{g}", kt))
                        act.activation(PT[tt][:, kt, :], tile(f"PT{tt}_{g}", kt)[:, :], ACT.Copy).then_inc(drained["A"], 1)
                    act.wait_ge(psum_full, filled(f"O{tt}_{g}"))
                    act.activation(attn_T[:, GQ * g:GQ * (g + 1), tt * P:(tt + 1) * P],
                                   tile(f"O{tt}_{g}")[:, :].rearrange("p (a b) -> p a b", a=GQ), ACT.Copy).then_inc(drained["A"], 1)

            for c in range(3):
                projected(c)
            for i in range(0, 9, 2):
                act.wait_ge(psum_full, filled("qiT", i))
                n = 2 if i < 8 else 1
                act.activation(qiT[0:IDH, 2 * i:2 * i + n, :].rearrange("p a b -> p (a b)"), tile("qiT", i)[0:IDH, 0:n * SEQ],
                               ACT.Copy).then_inc(drained["A"], 1)
            act.wait_ge(psum_full, filled("kT", 0))
            act.activation(qT[:, AH:AH + 2, :].rearrange("p a b -> p (a b)"), tile("kT", 0)[:, :], ACT.Copy).then_inc(drained["A"], 1)
            for c in (3, 4):
                projected(c)
            heads_in(0)
            projected(5)
            heads_in(1)
            projected(V_CHUNK)
            heads_out(0)
            heads_in(2)
            projected(7)
            heads_out(1)
            heads_in(3)

            def attn_hi(g):
                t = first[f"O1_{g}"]
                act.wait_ge(drained["A"], drained_by[:t + 1].count("A"))
                act.activation(x_hi[:, GQ * g:GQ * (g + 1), :], attn_T[:, GQ * g:GQ * (g + 1), :], ACT.Copy)\
                   .then_inc(out_hi_ready[1], 1)

            act.wait_ge(psum_full, filled("chunk1_7", 1))
            attn_hi(0)
            attn_hi(1)
            heads_out(2)
            attn_hi(2)
            act.wait_ge(psum_full, filled("S1_3", 1))
            act.wait_ge(drained["D"], drained_by[:first["S1_3"] + 2].count("D"))
            weight_hi(1, 0)
            heads_out(3)
            attn_hi(3)
            for q in range(1, 16):
                weight_hi(1, q)
            experts(1)

        @block.vector
        def _(v):
            step = [0]

            def link(ins):
                step[0] += 1
                ins.then_inc(dve, 1)
                v.wait_ge(dve, step[0])

            def hT_tiles(stage):
                for i in range(1, 8, 2):
                    v.wait_ge(psum_full, filled(stage, i))
                    v.tensor_copy(hT[:, 4 * (i % 4):4 * (i % 4) + 4, (i // 4) * P:(i // 4 + 1) * P],
                                  tile(stage, i)[:, :].rearrange("p (a b) -> p a b", a=4))\
                     .then_inc(drained["D"], 1)

            v.wait_ge(consts_ready, 1)
            hT_tiles("xT0")
            v.wait_ge(psum_full, filled("rows"))
            link(v.tensor_copy(small_cols[:, :], tile("rows")[:, 0:TAPS * 8 + 4]))
            v.engine_nop().then_inc(drained["D"], 1)
            v.wait_ge(psum_full, filled("gates", 0))
            v.wait_ge(small_loaded, 16 * 12)
            r = row
            v.memset(r["one"], 1.0)
            v.tensor_copy(t3[0:RANK, 0:SEQ], tile("gates")[64:64 + RANK, 0:SEQ])
            v.tensor_scalar(r["ig"], tile("gates")[0:NH, 0:SEQ], gate_bias[0:NH, :], None, ALU.add)
            link(v.tensor_scalar(r["xf"], tile("gates")[32:32 + NH, 0:SEQ], gate_bias[32:32 + NH, :], None, ALU.add))
            v.engine_nop().then_inc(drained["D"], 1)
            v.engine_nop().then_inc(lf_abs, 1)
            v.wait_ge(lf_log, 1)
            link(v.scalar_tensor_tensor(r["lf"], r["xf"], 0.0, r["ab"], ALU.min, ALU.subtract))
            link(v.tensor_tensor_scan(r["b"], r["one"], r["lf"], 0.0, ALU.mult, ALU.add))
            link(v.tensor_tensor(r["g"], r["ig"], r["b"], ALU.subtract))
            link(v.tensor_tensor_scan(r["M"], r["g"], r["g"], 0.0, ALU.max, ALU.max))
            v.tensor_scalar(r["nM"], r["M"], -1.0, None, ALU.mult)
            v.tensor_tensor(r["m"], r["b"], r["M"], ALU.add).then_inc(rows_done, 1)
            for c in range(2):
                for j in range(4):
                    n = 4 * c + j
                    v.wait_ge(psum_full, filled(f"chunk0_{c}", j))
                    src = tile(f"chunk0_{c}", j)
                    tap = [small_cols[:, t * 8 + n:t * 8 + n + 1] for t in range(TAPS)]
                    link(v.tensor_scalar(QKT[:, n, :], src[:, 0:SEQ], tap[TAPS - 1], None, ALU.mult))
                    for back in range(1, TAPS):
                        dst = QKT[:, n, back:SEQ]
                        ins = v.scalar_tensor_tensor(dst, src[:, 0:SEQ - back], tap[TAPS - 1 - back], dst, ALU.mult, ALU.add)
                        if back < TAPS - 1:
                            link(ins)
                        else:
                            ins.then_inc(drained["D"], 1)
                    v.wait_ge(drained["D"], drained_by[:first[f"chunk0_{c}"] + j + 1].count("D"))
                    v.engine_nop().then_inc(conv_done, 1)
            for i in range(2):
                v.wait_ge(psum_full, filled("decay", i))
                for j in range(2):
                    hd = 2 * i + j
                    ins = v.tensor_scalar(t1[:, hd * SEQ:(hd + 1) * SEQ], tile("decay", i)[:, j * SEQ:(j + 1) * SEQ],
                                          small_cols[:, 32 + hd:33 + hd], None, ALU.add)
                ins.then_inc(drained["D"], 1)
            v.wait_ge(drained["D"], drained_by[:first["decay"] + 2].count("D"))
            v.engine_nop().then_inc(gla_x, 1)
            v.wait_ge(psum_full, filled("gcols"))
            v.tensor_copy(gcol[:, :, :], tile("gcols")[:, :].rearrange("p (a b) -> p a b", a=4)[:, :, 0:NH]).then_inc(drained["D"], 1)
            v.wait_ge(drained["D"], drained_by[:first["gcols"] + 1].count("D"))
            v.engine_nop().then_inc(cols_done, 1)
            v.wait_ge(gla_log, 1)
            link(v.scalar_tensor_tensor(t1[:, :], t1[:, :], 0.0, t2[:, :], ALU.min, ALU.subtract))
            link(v.tensor_tensor_scan(la[:, :], resets[:, :], t1[:, :], 0.0, ALU.mult, ALU.add))
            v.tensor_scalar(la_last[:, :], la[:, :].rearrange("p (n c) -> p n c", c=CH)[:, :, CH - 1], 1.0 / 16, None, ALU.mult)\
             .then_inc(la_done, 1)
            flat = QKT[:, :, :].rearrange("p a b -> p (a b)")
            gq, gk = flat[:, 8 * SEQ:12 * SEQ], flat[:, 12 * SEQ:16 * SEQ]
            t = first["chunk0_3"] + 3
            v.wait_ge(drained["A"], drained_by[:t + 1].count("A"))
            v.wait_ge(gla_exp, 1)
            v.tensor_tensor(gq, gq, t1[:, :], ALU.mult).then_inc(qdec_done, 1)
            v.wait_ge(gla_exp, 3)
            v.tensor_tensor(t3[:, :], t3[:, :], gk, ALU.mult).then_inc(kend_done, 1)
            v.tensor_tensor(gk, gk, t2[:, :], ALU.mult).then_inc(qdec_done, 1)

            def mlstm_weights(hd):
                v.wait_ge(psum_full, filled(f"mS{hd}", 0))
                if hd >= 2:
                    v.wait_ge(psum_full, filled(f"mO{hd - 2}", 1))
                mb = tile(f"mS{hd}", 0)
                d = Dl[:, hd % 2, :]
                v.tensor_tensor(d[:, 0:SEQ], mb[:, 0:SEQ], maskT[:, :], ALU.add)
                link(v.tensor_tensor(d[:, SEQ:SEQ + P], mb[:, P:2 * P], maskT[:, 0:P], ALU.add))
                v.engine_nop().then_inc(drained["D"], 1)
                v.engine_nop().then_inc(D_ready, 1)
                v.wait_ge(psum_full, filled(f"mS{hd}", 1))
                v.wait_ge(E_ready, hd + 1)
                link(v.scalar_tensor_tensor(W[:, hd % 2, :], tile(f"mS{hd}", 1)[:, 0:384], DK ** -0.5, d, ALU.mult, ALU.mult))
                v.engine_nop().then_inc(drained["D"], 1)
                v.engine_nop().then_inc(W_ready, 1)

            def mlstm_normalise(hd):
                for tt in range(TT):
                    v.wait_ge(psum_full, filled(f"mO{hd}", tt))
                    t = tile(f"mO{hd}", tt)
                    link(v.tensor_scalar(den_r[:, 2:3], t[:, DV:DV + 1], -1.0, None, ALU.mult))
                    link(v.scalar_tensor_tensor(den_r[:, 0:1], t[:, DV:DV + 1], gcol[:, 2 + tt, hd:hd + 1], den_r[:, 2:3], ALU.max, ALU.max))
                    link(v.reciprocal(den_r[:, 1:2], den_r[:, 0:1]))
                    link(v.tensor_scalar(hn[:, tt * NH + hd, :], t[:, 0:DV], den_r[:, 1:2], None, ALU.mult))
                    v.engine_nop().then_inc(drained["D"], 1)
                    v.engine_nop().then_inc(hn_ready, 1)

            def head_norm(br):
                sl = slice(br * TT * NH, (br + 1) * TT * NH)
                v.tensor_scalar(ssq_m[:, sl], ssq[:, sl], 1.0 / DV, HN_EPS, ALU.mult, ALU.add).then_inc(ssq_scaled, 1)
                v.wait_ge(hr_ready, br + 1)
                for n in range(TT * NH):
                    g = norm_g[:, br * 1024 + (n % NH) * DV:br * 1024 + (n % NH + 1) * DV]
                    ins = v.scalar_tensor_tensor(hn[:, n, :], hn[:, n, :], hn_r[:, br * 8 + n:br * 8 + n + 1], g, ALU.mult, ALU.mult)
                link(ins)
                hn_t = hn[:, :, :].rearrange("p (t h) d -> p t (h d)", t=TT)
                for half in range(2):
                    v.wait_ge(gates_done, 1 + br * (1 + half))
                    m = mix[:, :, br * 1024 + half * 512:br * 1024 + (half + 1) * 512]
                    ins = v.tensor_tensor(m, m, hn_t[:, :, half * 512:(half + 1) * 512], ALU.mult)
                ins.then_inc(mlstm_mixed if br == 0 else mix_ready, 1)

            mlstm_weights(0)
            for hd in range(1, NH):
                mlstm_normalise(hd - 1)
                mlstm_weights(hd)
            mlstm_normalise(NH - 1)
            v.memset(kz[:, :, :, :].rearrange("p a b c -> p (a b c)"), 0.0).then_inc(kz_zero, 1)
            for c in range(3):
                for hp in range(2):
                    i = 2 * c + hp
                    v.wait_ge(psum_full, filled("gstate", i))
                    for j in range(2):
                        hd = 2 * hp + j
                        src = tile("gstate", i)[:, j * DV:(j + 1) * DV]
                        if c == 0:
                            ins = v.tensor_copy(state[:, 0, hd, :], src)
                        else:
                            ins = v.scalar_tensor_tensor(state[:, c, hd, :], state[:, c - 1, hd, :],
                                                         decay[:, hd * 4 + c:hd * 4 + c + 1], src, ALU.mult, ALU.add)
                    link(ins)
                    v.engine_nop().then_inc(drained["D"], 1)
                    v.engine_nop().then_inc(state_ready, 1)
            link(v.memset(attnT[:, :, :].rearrange("p a b -> p (a b)"), 0.0))
            for tt in range(TT):
                v.wait_ge(psum_full, filled("gattn", tt))
                link(v.copy_predicated(attnT[:, tt * NH:(tt + 1) * NH, :], chunk_mask.unsqueeze(1).broadcast_to([P, NH, P]),
                                       tile("gattn", tt)[:, :].rearrange("p (a b) -> p a b", a=NH)))
                v.engine_nop().then_inc(drained["D"], 1)
                v.engine_nop().then_inc(attn_ready, 1)
            v.wait_ge(ssq_ready, TT * NH)
            head_norm(0)
            def weight_lo(lay, q):
                v.wait_ge(w_hi_ready, 16 * lay + q + 1)
                n, w, lo = weight_quarter(lay, q)
                v.tensor_tensor(lo, w, w_hi[:, q % 2, :].bitcast(FP32), ALU.subtract).then_inc(w_lo_ready, 1)

            for q in range(2):
                weight_lo(0, q)
            v.wait_ge(ssq_ready, TT * NH + 4)
            t = first["gO"] + 3
            v.wait_ge(drained["A"], drained_by[:t + 1].count("A"))
            head_norm(1)
            for i in range(8):
                cols = (slice(None), slice(4 * (i % 4), 4 * (i % 4) + 4), slice((i // 4) * P, (i // 4 + 1) * P))
                v.wait_ge(out_hi_ready[0], i + 1)
                v.tensor_tensor(x_lo[cols], tile("mixT0", i)[:, :].rearrange("p (a b) -> p a b", a=4), x_hi[cols].bitcast(FP32), ALU.subtract)\
                 .then_inc(drained["D"], 1)

            def residual(lay):
                for c in range(4):
                    for q in range(4 * c + 2, min(4 * c + 6, 16)):
                        weight_lo(lay, q)
                    for tt in range(TT):
                        i = 2 * c + tt
                        v.wait_ge(psum_full, filled(f"out{lay}", i))
                        d = h[:, tt, c * BANK:(c + 1) * BANK]
                        v.scalar_tensor_tensor(d, d, ALPHA, tile(f"out{lay}", i)[:, :], ALU.mult, ALU.add).then_inc(drained["D"], 1)
                        v.wait_ge(drained["D"], drained_by[:first[f"out{lay}"] + i + 1].count("D"))
                        ins = v.bn_stats(stats[:, tt, c, :], d)
                link(ins)

            def layer_norm(n, src):
                for tt in range(TT):
                    ins = v.bn_aggr(mean_var[:, tt, :], stats[:, tt, :, :].rearrange("p a b -> p (a b)"))
                link(ins)
                v.tensor_scalar(var_eps[:, :], mean_var[:, :, 1], LN_EPS, None, ALU.add).then_inc(var_ready, 1)
                v.wait_ge(rstd_ready, n + 1)
                v.wait_ge(ln_loaded, 32 * (n + 1))
                for tt in range(TT):
                    link(v.scalar_tensor_tensor(h[:, tt, :], src[:, tt, :], mean_var[:, tt, 0:1], ln_gb[:, 0, :], ALU.subtract, ALU.mult))
                    v.scalar_tensor_tensor(h[:, tt, :], h[:, tt, :], rstd[:, tt:tt + 1], ln_gb[:, 1, :], ALU.mult, ALU.add)\
                     .then_inc(h_ready, 1)
                v.wait_ge(h_ready, TT * (n + 1))

            def ranks(jobs):
                def fours(x):
                    return x.rearrange("p t (g e) -> p (t g) e", e=4)

                jobs = [tuple(fours(x) for x in job) for job in jobs]
                for dst, _, _, _ in jobs:
                    ins = v.memset(dst, 0.0)
                link(ins)
                for shift in range(1, 4):
                    n = 4 - shift
                    for _, src, later, earlier in jobs:
                        v.tensor_tensor(later[:, :, 0:n], src[:, :, shift:4], src[:, :, 0:n], ALU.is_gt)
                        ins = v.tensor_tensor(earlier[:, :, 0:n], src[:, :, 0:n], src[:, :, shift:4], ALU.is_ge)
                    link(ins)
                    for dst, _, later, _ in jobs:
                        ins = v.tensor_tensor(dst[:, :, 0:n], dst[:, :, 0:n], later[:, :, 0:n], ALU.add)
                    link(ins)
                    for dst, _, _, earlier in jobs:
                        ins = v.tensor_tensor(dst[:, :, shift:4], dst[:, :, shift:4], earlier[:, :, 0:n], ALU.add)
                    link(ins)

            def experts(lay):
                s = M[lay]
                hT_tiles(f"moeT{lay}")
                v.memset(pick_w[:, :, :, :].rearrange("p a b c -> p (a b c)"), 0.0)
                v.tensor_scalar(acc[:, :, :].rearrange("p a b -> p (a b)"), h[:, :, :].rearrange("p a b -> p (a b)"), ALPHA, None, ALU.mult)
                v.wait_ge(psum_full, filled(f"route{lay}"))
                v.tensor_copy(logits_T[0:NE, :], tile(f"route{lay}")[0:NE, 0:SEQ]).then_inc(drained["D"], 1)
                v.wait_ge(psum_full, filled(f"route{lay}", 1))
                link(v.tensor_copy(aff[:, :, :].rearrange("p a b -> p (a b)"), tile(f"route{lay}", 1)[:, 0:TT * NE]))
                v.engine_nop().then_inc(drained["D"], 1)
                v.engine_nop().then_inc(logits_ready, 1)
                v.wait_ge(aff_ready, lay + 1)
                link(v.tensor_tensor(sel[:, :, :], aff[:, :, :], router_b[:, :].unsqueeze(1).broadcast_to([P, TT, NE]), ALU.add))
                s3 = sel[:, :, :].rearrange("p t (g e) -> p (t g) e", e=EPG)
                v.tensor_tensor(pairs6[:, :, 0:3], s3[:, :, 0:3], s3[:, :, 1:4], ALU.add)
                v.tensor_tensor(pairs6[:, :, 3:5], s3[:, :, 0:2], s3[:, :, 2:4], ALU.add)
                link(v.tensor_tensor(pairs6[:, :, 5:6], s3[:, :, 0:1], s3[:, :, 3:4], ALU.add))
                link(v.reduce_max(gsc[:, :, :].rearrange("p a b -> p (a b)"), pairs6[:, :, :], AX.X))
                ranks([(rank, sel, cmp, cmp2), (grank, gsc, gcmp, gcmp2)])
                link(v.tensor_scalar(cmp[:, :, 0:NG], grank[:, :, :], 0.5, None, ALU.is_lt))
                link(v.tensor_scalar(cmp2[:, :, :], rank[:, :, :], 1.5, None, ALU.is_lt))
                for tt in range(TT):
                    ins = v.tensor_tensor(chosen[:, tt, :].rearrange("p (g e) -> p g e", e=EPG),
                                          cmp2[:, tt, :].rearrange("p (g e) -> p g e", e=EPG),
                                          cmp[:, tt, 0:NG].unsqueeze(2).broadcast_to([P, NG, EPG]), ALU.mult)
                link(ins)
                v.engine_nop().then_inc(mask_ready, 1)
                link(v.tensor_tensor(sel[:, :, :], aff[:, :, :], chosen[:, :, :], ALU.mult))
                link(v.reduce_sum(csum[:, :, 0], sel[:, :, :], AX.X))
                link(v.reciprocal(crec[:, :, 0], csum[:, :, 0]))
                for tt in range(TT):
                    ins = v.tensor_scalar(sel[:, tt, :], sel[:, tt, :], crec[:, tt, :], None, ALU.mult)
                link(ins)
                v.wait_ge(psum_full, filled(f"pos{lay}"))
                t = tile(f"pos{lay}")
                link(v.scalar_tensor_tensor(rank[:, :, :], t[:, 0:2 * NE].rearrange("p (t e) -> p t e", t=TT), 1.0, chosen[:, :, :], ALU.add, ALU.mult))
                link(v.reduce_max(rounds_f[:, 0:1], t[:, 2 * NE:3 * NE], AX.X))
                v.engine_nop().then_inc(drained["D"], 1)
                for r_ in range(MAX_ROUNDS):
                    v.tensor_scalar(pos_r[:, :, r_ * NE:(r_ + 1) * NE], rank[:, :, :], -1.0 - CAP * r_, None, ALU.add)
                    v.tensor_copy(comb_r[:, :, r_ * NE:(r_ + 1) * NE], sel[:, :, :])
                link(v.tensor_scalar(rounds_f[:, 1:2], rounds_f[:, 0:1], CAP + 0.5, None, ALU.is_gt))
                for r_ in range(2, MAX_ROUNDS):
                    link(v.tensor_scalar(rounds_f[:, 2:3], rounds_f[:, 0:1], CAP * r_ + 0.5, None, ALU.is_gt))
                    link(v.tensor_tensor(rounds_f[:, 1:2], rounds_f[:, 1:2], rounds_f[:, 2:3], ALU.add))
                v.tensor_copy(rounds_i[:, :], rounds_f[:, 1:2]).then_inc(routed, 1)
                v.wait_ge(routed, lay + 1)
                n_r = v.value_load(rounds_i[0:1, 0:1], min_val=0, max_val=MAX_ROUNDS - 1) + 1

                def pick_tokens(pair):
                    for tt in range(TT):
                        for e in range(2):
                            ins = v.tensor_scalar(pick_p[:, tt, e * CAP:(e + 1) * CAP], slots64[:, :],
                                                  pos_r[:, tt, bass.ds(2 * pair + e, 1)], None, ALU.is_equal)
                    ins.then_inc(s["pick_ready"], 1)

                def add_tile(x, t8):
                    c, tt = t8 // 2, t8 % 2
                    v.wait_ge(s["sc_full"], 8 * x + t8 + 1)
                    d = acc[:, tt, c * BANK:(c + 1) * BANK]
                    v.tensor_tensor(d, ps[6 + t8 % 2][:, :], d, ALU.add).then_inc(s["sc_drained"], 1)

                def expert(q, i, is_first, is_last):
                    x = 2 * q + i
                    begun = not (is_first and i == 0)
                    if not is_first:
                        v.wait_ge(s["xc_full"], 6 * q + i - 1)
                    for tt in range(TT):
                        ins = v.tensor_scalar(pick_w[:, i, tt, CAP:2 * CAP], slots64[:, :], pos_r[:, tt, bass.ds(x, 1)],
                                              comb_r[:, tt, bass.ds(x, 1)], ALU.is_equal, ALU.mult)
                    ins.then_inc(s["pw_ready"], 1)
                    if i == 0 and not is_last:
                        v.wait_ge(s["xc_full"], 6 * q + 4)
                        pick_tokens(q + 1)
                    v.wait_ge(s["up_full"], x + 1)
                    v.wait_ge(s["silu_ready"], x + 1)
                    if begun:
                        v.wait_ge(s["hT_full"], x)
                    v.tensor_tensor(h_e[:, :], ps[1][:, 0:DV], silu_g[:, :], ALU.mult).then_inc(s["h_ready"], 1)
                    if begun:
                        for t8 in range(8):
                            add_tile(x - 1, t8)

                pick_tokens(0)
                for i in range(2):
                    expert(0, i, True, False)
                with v.Fori(1, n_r * PAIRS - 1) as q:
                    for i in range(2):
                        expert(q, i, False, False)
                q = n_r * PAIRS - 1
                for i in range(2):
                    expert(q, i, False, True)
                for t8 in range(8):
                    c, tt = t8 // 2, t8 % 2
                    add_tile(2 * q + 1, t8)
                    v.wait_ge(s["sc_drained"], 16 * q + 9 + t8)
                    ins = v.bn_stats(stats[:, tt, c, :], acc[:, tt, c * BANK:(c + 1) * BANK])
                link(ins)

            residual(0)
            layer_norm(0, h)
            experts(0)
            layer_norm(1, acc)

            for half, at in ((16, 0), (8, 16)):
                f = np.float32(1) / (np.float32(500000.0) ** (np.arange(half, dtype=np.float32) / np.float32(half)))
                for n in range(half):
                    ins = v.memset(freq[:, at + n:at + n + 1], float(f[n]))
            link(v.tensor_copy(pos_f[:, :], pos_int[:, :]))
            for tt in range(TT):
                ins = v.tensor_scalar(angles[:, tt, :], freq[:, :], pos_f[:, tt:tt + 1], None, ALU.mult)
            link(ins)
            ang = angles[:, :, :].rearrange("p a b -> p (a b)")
            two_pi = 2 * math.pi
            c1 = 6.28125
            c2 = float(np.float32(round((two_pi - c1) * 2 ** 21) / 2 ** 21))
            c3 = float(np.float32(two_pi - c1 - c2))
            magic = 1.5 * 2 ** 23
            turn = [score[:, 0, 0:48], score[:, 0, 48:96]]
            for n, quarter in enumerate((0.0, 0.25)):
                v.tensor_scalar(turn[n], ang, float(np.float32(1 / two_pi)), quarter, ALU.mult, ALU.add)
            link(v.engine_nop())
            for n in range(2):
                ins = v.tensor_scalar(turn[n], turn[n], magic, None, ALU.add)
            link(ins)
            for n in range(2):
                ins = v.tensor_scalar(turn[n], turn[n], magic, None, ALU.subtract)
            link(ins)
            for m, cc in enumerate((c1, c2, c3)):
                for n in range(2):
                    ins = v.scalar_tensor_tensor(kf[:, n, :], turn[n], -cc, ang if m == 0 else kf[:, n, :], ALU.mult, ALU.add)
                link(ins)
            link(v.tensor_scalar(kf[:, 1, :], kf[:, 1, :], math.pi / 2, None, ALU.add))
            v.tensor_scalar(kf[:, :, :].rearrange("p a b -> p (a b)"), kf[:, :, :].rearrange("p a b -> p (a b)"), 3.1415925, -3.1415925, ALU.min, ALU.max)\
             .then_inc(trig_in, 1)
            hT_tiles("xT1")
            v.wait_ge(psum_full, filled("small1"))
            v.tensor_copy(small_T, tile("small1")[0:IDH + IH, 0:SEQ]).then_inc(drained["D"], 1)
            v.wait_ge(psum_full, filled("small1T"))
            for tt in range(TT):
                v.tensor_copy(QIN[:, tt, IH, :], tile("small1T")[:, tt * P:tt * P + IDH])
                ins = v.tensor_scalar(wi[:, tt, :], tile("small1T")[:, tt * P + IDH:tt * P + 80], float(IH ** -0.5 * IDH ** -0.5), None, ALU.mult)
            ins.then_inc(drained["D"], 1)
            v.wait_ge(trig_out, 1)

            def rope(x, tmp_at, n_before, half, at):
                if n_before:
                    v.wait_ge(roped, n_before)
                heads = x.shape[2]
                x1, x2 = x[:, :, :, 0:half], x[:, :, :, half:2 * half]

                def tmp(n, tt):
                    return tmp_at[:, n, tt * heads * half:(tt + 1) * heads * half].rearrange("p (a b) -> p a b", b=half)

                for tt in range(TT):
                    c = cosv[:, tt, at:at + half].unsqueeze(1).broadcast_to([P, heads, half])
                    s_ = sinv[:, tt, at:at + half].unsqueeze(1).broadcast_to([P, heads, half])
                    v.tensor_tensor(tmp(0, tt), x1[:, tt], c, ALU.mult)
                    v.tensor_tensor(tmp(1, tt), x2[:, tt], s_, ALU.mult)
                    v.tensor_tensor(tmp(2, tt), x2[:, tt], c, ALU.mult)
                    ins = v.tensor_tensor(tmp(3, tt), x1[:, tt], s_, ALU.mult)
                link(ins)
                for tt in range(TT):
                    v.tensor_tensor(x1[:, tt], tmp(0, tt), tmp(1, tt), ALU.subtract)
                    ins = v.tensor_tensor(x2[:, tt], tmp(2, tt), tmp(3, tt), ALU.add)
                ins.then_inc(roped, 1)

            def wait_projected(c):
                t = first[f"chunk1_{c}"] + 1
                v.wait_ge(drained["A"], drained_by[:t + 1].count("A"))

            wait_projected(1)
            v.wait_ge(drained["D"], drained_by[:first["small1T"] + 1].count("D"))
            rope(QIN, rope_t, 0, IDH // 8, 16)
            wait_projected(2)
            rope(QN[:, :, AH:AH + KVH, :], rope_t, 1, DH // 8, 0)
            for i in range(1, 9, 2):
                v.wait_ge(psum_full, filled("qiT", i))
                v.tensor_copy(qiT[0:IDH, 2 * i:2 * i + 2, :].rearrange("p a b -> p (a b)"), tile("qiT", i)[0:IDH, :])\
                 .then_inc(drained["D"], 1)
            v.wait_ge(roped, 2)
            for tt, lo, hi in ((1, 0, 8), (0, 8, 12)):
                nk = P * (tt + 1)
                per = BANK // nk
                for i in range(lo, hi):
                    v.wait_ge(psum_full, filled("index", i))
                    h0 = per * (i - lo)
                    v.scalar_tensor_tensor(R[:, h0:h0 + per, 0:nk], tile("index", i)[:, :].rearrange("p (a b) -> p a b", a=per), 0.0,
                                           wi[:, tt, h0:h0 + per].unsqueeze(2).broadcast_to([P, per, nk]), ALU.max, ALU.mult)\
                     .then_inc(drained["D"], 1)
                v.wait_ge(drained["D"], drained_by[:first["index"] + hi].count("D"))
                link(v.reduce_sum(score[:, tt, 0:nk], R[:, :, 0:nk].rearrange("p a b -> p b a"), AX.X))
                link(v.tensor_tensor(work[:, tt, 0:nk], score[:, tt, 0:nk], maskN[:, SEQ - nk:SEQ], ALU.add))
            v.wait_ge(psum_full, filled("kT", 1))
            v.tensor_copy(qT[:, AH + 2:AH + 4, :].rearrange("p a b -> p (a b)"), tile("kT", 1)[:, :]).then_inc(drained["D"], 1)
            for _ in range(TOPK // 8):
                for tt in range(TT):
                    ins = v.max(top8[:, tt, :], work[:, tt, 0:P * (tt + 1)])
                link(ins)
                for tt in range(TT):
                    w_ = work[:, tt, 0:P * (tt + 1)]
                    ins = v.match_replace(w_, top8[:, tt, :], w_, TAKEN)
                link(ins)
            for tt in range(TT):
                w_ = work[:, tt, 0:P * (tt + 1)]
                ins = v.tensor_scalar(w_, w_, TAKEN / 2, NEG, ALU.is_gt, ALU.mult)
            link(ins)
            for tt in range(TT):
                w_ = work[:, tt, 0:P * (tt + 1)]
                ins = v.tensor_tensor(w_, w_, maskN[:, SEQ - P * (tt + 1):SEQ], ALU.add)
            link(ins)
            for g in range(KVH):
                wait_projected(Q_CHUNK[g])
                rope(QN[:, :, GQ * g:GQ * (g + 1), :], rope_q, 2 + g, DH // 8, 0)
                v.wait_ge(psum_full, filled(f"qT{g}", 1))
                v.tensor_copy(qT[:, GQ * g + 2:GQ * g + 4, :].rearrange("p a b -> p (a b)"), tile(f"qT{g}", 1)[:, :])\
                 .then_inc(drained["D"], 1)
                for tt in range(TT):
                    nk = P * (tt + 1)
                    per = BANK // nk
                    x = X[g % 2][tt]
                    for i in range(GQ // per):
                        v.wait_ge(psum_full, filled(f"S{tt}_{g}", i))
                        v.scalar_tensor_tensor(x[:, per * i:per * (i + 1), :],
                                               tile(f"S{tt}_{g}", i)[:, :].rearrange("p (a b) -> p a b", a=per), DH ** -0.5,
                                               work[:, tt, 0:nk].unsqueeze(1).broadcast_to([P, per, nk]), ALU.mult, ALU.add)\
                         .then_inc(drained["D"], 1)
                    v.wait_ge(drained["D"], drained_by[:first[f"S{tt}_{g}"] + GQ // per].count("D"))
                    link(v.reduce_max(mx[:, tt, 0:GQ], x, AX.X))
                    v.tensor_scalar(mx[:, tt, GQ:2 * GQ], mx[:, tt, 0:GQ], -1.0, None, ALU.mult).then_inc(X_ready, 1)
                for tt in range(TT):
                    v.wait_ge(exp_ready, TT * g + tt + 1)
                    link(v.reciprocal(mx[:, tt, 0:GQ], mx[:, tt, 2 * GQ:3 * GQ]))
                    for j in range(GQ):
                        x = X[g % 2][tt][:, j, :]
                        ins = v.tensor_scalar(x, x, mx[:, tt, j:j + 1], None, ALU.mult)
                    ins.then_inc(P_ready, 1)
            def attn_lo(g):
                v.wait_ge(out_hi_ready[1], g + 1)
                heads = slice(GQ * g, GQ * (g + 1))
                v.tensor_tensor(x_lo[:, heads, :], attn_T[:, heads, :], x_hi[:, heads, :].bitcast(FP32), ALU.subtract)\
                 .then_inc(attn_lo_ready, 1)

            for g in range(3):
                attn_lo(g)
            weight_lo(1, 0)
            v.wait_ge(psum_full, filled("O1_3"))
            t = first["out1"] - 1
            v.wait_ge(drained["A"], drained_by[:t + 1].count("A"))
            v.engine_nop().then_inc(mixer1_done, 1)
            attn_lo(3)
            weight_lo(1, 1)
            residual(1)
            layer_norm(2, h)
            experts(1)
            layer_norm(3, acc)


_INS = ["x", "positions", "ab_w_in", "ab_conv_w", "ab_igate_b", "ab_fgate_b", "ab_gla_gate_w2", "ab_gla_gate_b",
        "ab_mlstm_norm_g", "ab_gla_norm_g", "ab_w_out", "c_w_in", "c_w_out", "router_w", "router_bias",
        "moe_w_gate", "moe_w_up", "moe_w_down", "ln_mix_g", "ln_mix_b", "ln_ffn_g", "ln_ffn_b"]


def kernel(**inputs):
    import numpy as _np
    import concourse.bacc as _bacc
    from concourse import mybir as _mybir
    from concourse.bass_utils import run_bass_kernel_spmd as _run

    nc = _bacc.Bacc("TRN2", target_bir_lowering=False, num_devices=1)
    arrays, aps = {}, {}
    for name in _INS:
        x = _np.ascontiguousarray(inputs[name])
        arrays[f"in_{name}"] = x
        aps[name] = nc.dram_tensor(f"in_{name}", x.shape, _mybir.dt.from_np(x.dtype), kind="ExternalInput").ap()
    out = nc.dram_tensor("out", (1, SEQ, D), _mybir.dt.float32, kind="ExternalOutput").ap()
    program(nc, aps, out)
    r = _run(nc, [arrays], core_ids=[0])
    return r.results[0]["out"]
```
